# Optimizing a Trainium2 kernel written in Bass

```python
import math
import jax, jax.numpy as jnp
from jax import lax
import numpy as np

D_MODEL = 2048
BATCH = 1
SEQ = 256
DEPTH = 2

CHUNK = 64
Q_BLOCK = 128
ROPE_THETA = 500000.0
NORM_EPS = 1e-6
NEG_INF = -1e30
PLE_DIM = 256
HEAD_DIM = 128

A_HEADS = 6
A_Q_RANK = 384
A_KV_RANK = 256
A_NOPE = 128
A_ROPE = 64
A_V = 128
A_WIDTH = A_HEADS * A_V
B_HEADS = 5
B_WIDTH = B_HEADS * HEAD_DIM
IDX_HEADS = 8
IDX_DIM = 64
TOPK_MAX = 256
C_HEADS = 5
C_QK = 64
C_V = 128
C_WIDTH = C_HEADS * C_V
D_MIX = A_WIDTH + B_WIDTH + C_WIDTH

IN_SPLITS = (A_Q_RANK, A_KV_RANK, A_ROPE, A_WIDTH,
             B_WIDTH, B_WIDTH, B_WIDTH, IDX_HEADS * IDX_DIM, IDX_DIM, IDX_HEADS, B_WIDTH,
             C_HEADS * 2 * C_QK, C_HEADS * 2 * C_QK, C_WIDTH, C_WIDTH)
D_IN = sum(IN_SPLITS)


def rms_norm(x, g):
    xf = x.astype(jnp.float32)
    y = xf * lax.rsqrt(jnp.mean(xf * xf, axis=-1, keepdims=True) + NORM_EPS)
    return (y * g.astype(jnp.float32)).astype(x.dtype)

def rope(x, pos, n_rot):
    half = n_rot // 2
    inv_freq = 1.0 / (ROPE_THETA ** (jnp.arange(half, dtype=jnp.float32) * (2.0 / n_rot)))
    ang = pos.astype(jnp.float32)[:, :, None] * inv_freq
    cos = jnp.cos(ang)[:, :, None, :]
    sin = jnp.sin(ang)[:, :, None, :]
    x1 = x[..., :half].astype(jnp.float32)
    x2 = x[..., half:n_rot].astype(jnp.float32)
    rot = jnp.concatenate([x1 * cos - x2 * sin, x2 * cos + x1 * sin], axis=-1).astype(x.dtype)
    return jnp.concatenate([rot, x[..., n_rot:]], axis=-1)

def split_cols(z, sizes):
    out, o = [], 0
    for sz in sizes:
        out.append(z[..., o:o + sz])
        o += sz
    return out

def to_blocks(a):
    b, s = a.shape[:2]
    return jnp.swapaxes(a.reshape(b, s // Q_BLOCK, Q_BLOCK, *a.shape[2:]), 0, 1)

def from_blocks(a):
    nb, b, qb = a.shape[:3]
    return jnp.swapaxes(a, 0, 1).reshape(b, nb * qb, *a.shape[3:])

def chunk_mask(blk, seq):
    q_pos = blk * Q_BLOCK + jnp.arange(Q_BLOCK)
    k_pos = jnp.arange(seq)
    return (k_pos // CHUNK)[None, :] <= (q_pos // CHUNK)[:, None]

def masked_softmax(scores, mask):
    return jax.nn.softmax(jnp.where(mask, scores.astype(jnp.float32), NEG_INF), axis=-1)

def mla_mixer(c_q, c_kv, k_rope, pos, q_norm_g, kv_norm_g, w_uq, w_ukv):
    b, s, _ = c_q.shape
    q = (rms_norm(c_q, q_norm_g) @ w_uq).reshape(b, s, A_HEADS, A_NOPE + A_ROPE)
    q = jnp.concatenate([q[..., :A_NOPE], rope(q[..., A_NOPE:], pos, A_ROPE)], axis=-1)
    kv = (rms_norm(c_kv, kv_norm_g) @ w_ukv).reshape(b, s, A_HEADS, A_NOPE + A_V)
    k_pe = rope(k_rope[:, :, None, :], pos, A_ROPE)
    k = jnp.concatenate([kv[..., :A_NOPE], jnp.broadcast_to(k_pe, (b, s, A_HEADS, A_ROPE))], axis=-1)
    v = kv[..., A_NOPE:]
    scale = (A_NOPE + A_ROPE) ** -0.5

    def block(args):
        blk, qb = args
        sc = jnp.einsum('bqhd,bkhd->bhqk', qb, k) * scale
        pr = masked_softmax(sc, chunk_mask(blk, s)).astype(v.dtype)
        return jnp.einsum('bhqk,bkhd->bqhd', pr, v)

    o = from_blocks(lax.map(block, (jnp.arange(s // Q_BLOCK), to_blocks(q))))
    return o.reshape(b, s, A_WIDTH)

def dsa_mixer(q, k, v, q_idx, k_idx, w_idx, pos):
    b, s, _ = q.shape
    q = rope(q.reshape(b, s, B_HEADS, HEAD_DIM), pos, HEAD_DIM // 4)
    k = rope(k.reshape(b, s, B_HEADS, HEAD_DIM), pos, HEAD_DIM // 4)
    v = v.reshape(b, s, B_HEADS, HEAD_DIM)
    qi = rope(q_idx.reshape(b, s, IDX_HEADS, IDX_DIM), pos, IDX_DIM // 4)
    ki = rope(k_idx[:, :, None, :], pos, IDX_DIM // 4)[:, :, 0, :]
    n_sel = min(TOPK_MAX, s // 4)
    scale = HEAD_DIM ** -0.5

    def block(args):
        blk, qb, qib, wb = args
        mask = chunk_mask(blk, s)
        rel = jax.nn.relu(jnp.einsum('bqhd,bkd->bqhk', qib, ki).astype(jnp.float32))
        score = jnp.einsum('bqhk,bqh->bqk', rel, wb.astype(jnp.float32))
        score = jnp.where(mask[None], score, NEG_INF)
        top_val, top_idx = lax.top_k(score, n_sel)
        valid = top_val > 0.5 * NEG_INF
        kg = jax.vmap(lambda kk, ii: kk[ii])(k, top_idx)
        vg = jax.vmap(lambda vv, ii: vv[ii])(v, top_idx)
        sc = jnp.einsum('bqhd,bqkhd->bhqk', qb, kg) * scale
        pr = masked_softmax(sc, valid[:, None]).astype(v.dtype)
        return jnp.einsum('bhqk,bqkhd->bqhd', pr, vg)

    o = from_blocks(lax.map(block, (jnp.arange(s // Q_BLOCK), to_blocks(q), to_blocks(qi), to_blocks(w_idx))))
    return o.reshape(b, s, B_WIDTH)

def diff_mixer(q, k, v, pos, lam, lam_init, subln_g):
    b, s, _ = q.shape
    q = rope(q.reshape(b, s, C_HEADS * 2, C_QK), pos, C_QK // 4).reshape(b, s, C_HEADS, 2, C_QK)
    k = rope(k.reshape(b, s, C_HEADS * 2, C_QK), pos, C_QK // 4).reshape(b, s, C_HEADS, 2, C_QK)
    v = v.reshape(b, s, C_HEADS, C_V)
    k1, k2 = k[..., 0, :], k[..., 1, :]
    scale = C_QK ** -0.5

    def block(args):
        blk, qb = args
        mask = chunk_mask(blk, s)
        a1 = masked_softmax(jnp.einsum('bqhd,bkhd->bhqk', qb[..., 0, :], k1) * scale, mask)
        a2 = masked_softmax(jnp.einsum('bqhd,bkhd->bhqk', qb[..., 1, :], k2) * scale, mask)
        pr = (a1 - lam * a2).astype(v.dtype)
        return jnp.einsum('bhqk,bkhd->bqhd', pr, v)

    o = from_blocks(lax.map(block, (jnp.arange(s // Q_BLOCK), to_blocks(q))))
    o = rms_norm(o, subln_g) * (1.0 - lam_init)
    return o.reshape(b, s, C_WIDTH)

def first_inputs(seed: int = 0) -> dict:
    key = jax.random.key(seed)
    ks = jax.random.split(key, 20)
    f32 = jnp.float32
    nrm = lambda k, shape, sc: jax.random.normal(k, shape, f32) * sc
    x = nrm(ks[0], (BATCH, SEQ, D_MODEL), 1.0)
    p = nrm(ks[1], (DEPTH, BATCH, SEQ, PLE_DIM), 1.0)
    start = jax.random.randint(ks[2], (BATCH, 1), 0, 64, dtype=jnp.int32) * CHUNK
    positions = (start + jnp.arange(SEQ, dtype=jnp.int32)[None, :]).astype(jnp.int32)
    return {
        "x": x,
        "p": p,
        "positions": positions,
        "w_in": nrm(ks[3], (DEPTH, D_MODEL, D_IN), D_MODEL ** -0.5),
        "w_uq": nrm(ks[4], (DEPTH, A_Q_RANK, A_HEADS * (A_NOPE + A_ROPE)), A_Q_RANK ** -0.5),
        "w_ukv": nrm(ks[5], (DEPTH, A_KV_RANK, A_HEADS * (A_NOPE + A_V)), A_KV_RANK ** -0.5),
        "w_o": nrm(ks[6], (DEPTH, D_MIX, D_MODEL), D_MIX ** -0.5),
        "norm_g": 1.0 + nrm(ks[7], (DEPTH, D_MODEL), 0.02),
        "q_norm_g": 1.0 + nrm(ks[8], (DEPTH, A_Q_RANK), 0.02),
        "kv_norm_g": 1.0 + nrm(ks[9], (DEPTH, A_KV_RANK), 0.02),
        "lam_q1": nrm(ks[10], (DEPTH, C_QK), 0.1),
        "lam_k1": nrm(ks[11], (DEPTH, C_QK), 0.1),
        "lam_q2": nrm(ks[12], (DEPTH, C_QK), 0.1),
        "lam_k2": nrm(ks[13], (DEPTH, C_QK), 0.1),
        "subln_g": 1.0 + nrm(ks[14], (DEPTH, C_V), 0.02),
        "w_ple": nrm(ks[15], (DEPTH, PLE_DIM, D_MODEL), PLE_DIM ** -0.5),
        "w_pg": nrm(ks[16], (DEPTH, D_MODEL, D_MODEL), D_MODEL ** -0.5),
        "final_g": 1.0 + nrm(ks[17], (D_MODEL,), 0.02),
    }

def first_block(x, p, positions, w_in, w_uq, w_ukv, w_o, norm_g, q_norm_g, kv_norm_g,
              lam_q1, lam_k1, lam_q2, lam_k2, subln_g, w_ple, w_pg, final_g):
    h = x
    f32 = jnp.float32
    for i in range(DEPTH):
        u = rms_norm(h, norm_g[i])
        z = u @ w_in[i]
        (c_q, c_kv, k_rope, g_a,
         q_b, k_b, v_b, q_idx, k_idx, w_idx, g_b,
         q_c, k_c, v_c, g_c) = split_cols(z, IN_SPLITS)
        o_a = mla_mixer(c_q, c_kv, k_rope, positions, q_norm_g[i], kv_norm_g[i], w_uq[i], w_ukv[i])
        o_b = dsa_mixer(q_b, k_b, v_b, q_idx, k_idx, w_idx, positions)
        lam_init = 0.8 - 0.6 * math.exp(-0.3 * i)
        lam = (jnp.exp(jnp.sum(lam_q1[i].astype(f32) * lam_k1[i].astype(f32)))
               - jnp.exp(jnp.sum(lam_q2[i].astype(f32) * lam_k2[i].astype(f32))) + lam_init)
        o_c = diff_mixer(q_c, k_c, v_c, positions, lam, lam_init, subln_g[i])
        mixed = jnp.concatenate([o_a * jax.nn.silu(g_a),
                                 o_b * jax.nn.silu(g_b),
                                 o_c * jax.nn.silu(g_c)], axis=-1)
        h = h + mixed @ w_o[i]
        h = h + (p[i] @ w_ple[i]) * jax.nn.sigmoid(h @ w_pg[i])
    return rms_norm(h, final_g)


DEPTH_2 = 4

GRID_W = 64
CTX_LEN = 256
N_MIXERS = 3
D_BRANCH = D_MODEL
FOURIER_GROUPS = 8
HEAD_DIM_2 = 64
N_HEADS = D_BRANCH // HEAD_DIM_2
N_KV_HEADS = 4
GQA_GROUP = N_HEADS // N_KV_HEADS
WINDOW = 128
BLOCK = 128
BAND = 3 * BLOCK
ROPE_BASE = 10000.0
ATTN_SCALE = HEAD_DIM_2 ** -0.5
NEG_INF_2 = -1e30
ATTN_IN = (N_HEADS + 2 * N_KV_HEADS) * HEAD_DIM_2 + D_BRANCH
CONV_WIDTH = 31
N_FOURIER_LAYERS = (DEPTH_2 + 2) // 3
N_ATTN_LAYERS = (DEPTH_2 + 1) // 3
N_CONV_LAYERS = DEPTH_2 // 3


def rms_norm_2(x, g):
    xf = x.astype(jnp.float32)
    y = xf * lax.rsqrt(jnp.mean(xf * xf, axis=-1, keepdims=True) + NORM_EPS)
    return (y * g.astype(jnp.float32)).astype(x.dtype)

def layer_norm(x, g, b):
    xf = x.astype(jnp.float32)
    mu = jnp.mean(xf, axis=-1, keepdims=True)
    var = jnp.mean(jnp.square(xf - mu), axis=-1, keepdims=True)
    y = (xf - mu) * lax.rsqrt(var + NORM_EPS) * g.astype(jnp.float32) + b.astype(jnp.float32)
    return y.astype(x.dtype)

def ada_modulation(cond, w, b):
    m = jax.nn.silu(cond) @ w + b
    return jnp.split(m, 3, axis=-1)

def axial_rope_tables(n_tokens):
    rows = n_tokens // GRID_W
    row = jnp.repeat(jnp.arange(rows), GRID_W).astype(jnp.float32)
    col = jnp.tile(jnp.arange(GRID_W), rows).astype(jnp.float32)
    quarter = HEAD_DIM_2 // 4
    inv_freq = ROPE_BASE ** (-jnp.arange(quarter, dtype=jnp.float32) / quarter)
    ang_r = row[:, None] * inv_freq[None, :]
    ang_c = col[:, None] * inv_freq[None, :]
    ang = jnp.concatenate([ang_r, ang_r, ang_c, ang_c], axis=-1)
    return jnp.cos(ang), jnp.sin(ang)

def apply_rope(x, cos, sin):
    n = x.shape[1]
    bshape = (1, n) + (1,) * (x.ndim - 3) + (HEAD_DIM_2,)
    xf = x.astype(jnp.float32)
    xr = xf.reshape(x.shape[:-1] + (2, 2, HEAD_DIM_2 // 4))
    rot = jnp.stack([-xr[..., 1, :], xr[..., 0, :]], axis=-2).reshape(x.shape)
    return (xf * cos.reshape(bshape) + rot * sin.reshape(bshape)).astype(x.dtype)

def fourier_mix(h, w_in, w_out):
    b, n, _ = h.shape
    u, z = jnp.split(h @ w_in, 2, axis=-1)
    ug = u.reshape(b, n, FOURIER_GROUPS, D_BRANCH // FOURIER_GROUPS).astype(jnp.float32)
    mixed = jnp.fft.fft2(ug, axes=(1, 3), norm='ortho').real
    y = mixed.reshape(b, n, D_BRANCH).astype(h.dtype) * jax.nn.silu(z)
    return y @ w_out

def conformer_conv_mix(h, w_in, dw_w, dw_b, ln_g, ln_b, w_out):
    a, a_gate, z = jnp.split(h @ w_in, 3, axis=-1)
    g = a * jax.nn.sigmoid(a_gate)
    pad = CONV_WIDTH // 2
    y = lax.conv_general_dilated(
        g, dw_w[:, None, :].astype(g.dtype), window_strides=(1,),
        padding=[(pad, pad)], dimension_numbers=('NWC', 'WIO', 'NWC'),
        feature_group_count=D_BRANCH) + dw_b
    y = jax.nn.silu(layer_norm(y, ln_g, ln_b))
    return (y * jax.nn.silu(z)) @ w_out

def split_qkvz(h, w_in):
    b, n, _ = h.shape
    proj = h @ w_in
    q_end = N_HEADS * HEAD_DIM_2
    k_end = q_end + N_KV_HEADS * HEAD_DIM_2
    v_end = k_end + N_KV_HEADS * HEAD_DIM_2
    q = proj[..., :q_end].reshape(b, n, N_KV_HEADS, GQA_GROUP, HEAD_DIM_2)
    k = proj[..., q_end:k_end].reshape(b, n, N_KV_HEADS, HEAD_DIM_2)
    v = proj[..., k_end:v_end].reshape(b, n, N_KV_HEADS, HEAD_DIM_2)
    z = proj[..., v_end:]
    return q, k, v, z

def sink_softmax(s, sink):
    s_sink = jnp.broadcast_to(sink[None, :, :, None, None], s.shape[:-1] + (1,))
    p = jax.nn.softmax(jnp.concatenate([s, s_sink], axis=-1), axis=-1)
    return p[..., :-1]

def window_attention_mix(h, hc, w_in, sink, w_out, cos, sin, with_ctx_out):
    b, n, _ = h.shape
    n_ctx = hc.shape[1]
    n_blocks = n // BLOCK
    q, k, v, z = split_qkvz(h, w_in)
    qc, kc, vc, zc = split_qkvz(hc, w_in)
    q = apply_rope(q, cos, sin) * ATTN_SCALE
    k = apply_rope(k, cos, sin)
    sink = sink.reshape(N_KV_HEADS, GQA_GROUP).astype(jnp.float32)
    pad = ((0, 0), (BLOCK, BLOCK), (0, 0), (0, 0))
    kp = jnp.pad(k, pad)
    vp = jnp.pad(v, pad)
    q_off = jnp.arange(BLOCK)[:, None]
    k_off = jnp.arange(BAND)[None, :] - BLOCK
    rel_ok = jnp.abs(q_off - k_off) <= WINDOW

    def block(bi):
        start = bi * BLOCK
        qb = lax.dynamic_slice_in_dim(q, start, BLOCK, axis=1)
        kb = lax.dynamic_slice_in_dim(kp, start, BAND, axis=1)
        vb = lax.dynamic_slice_in_dim(vp, start, BAND, axis=1)
        kpos = start + k_off
        valid = rel_ok & (kpos >= 0) & (kpos < n)
        s_loc = jnp.einsum('bqhgd,bkhd->bhgqk', qb, kb).astype(jnp.float32)
        s_loc = jnp.where(valid, s_loc, NEG_INF_2)
        s_ctx = jnp.einsum('bqhgd,bkhd->bhgqk', qb, kc).astype(jnp.float32)
        p = sink_softmax(jnp.concatenate([s_loc, s_ctx], axis=-1), sink).astype(v.dtype)
        return (jnp.einsum('bhgqk,bkhd->bqhgd', p[..., :BAND], vb)
                + jnp.einsum('bhgqk,bkhd->bqhgd', p[..., BAND:], vc))

    o = lax.map(block, jnp.arange(n_blocks))
    o = jnp.moveaxis(o, 0, 1).reshape(b, n, D_BRANCH)
    out = (o * jax.nn.silu(z)) @ w_out
    if not with_ctx_out:
        return out, None
    s_c = jnp.einsum('bqhgd,bkhd->bhgqk', qc * ATTN_SCALE, kc).astype(jnp.float32)
    p_c = sink_softmax(s_c, sink).astype(vc.dtype)
    oc = jnp.einsum('bhgqk,bkhd->bqhgd', p_c, vc).reshape(b, n_ctx, D_BRANCH)
    out_c = (oc * jax.nn.silu(zc)) @ w_out
    return out, out_c

def second_inputs(seed: int = 0) -> dict:
    key = jax.random.key(seed)
    ks = jax.random.split(key, 20)
    f32 = jnp.float32

    def nrm(k, shape, s):
        return jax.random.normal(k, shape, f32) * s

    d, e = D_MODEL, D_BRANCH
    return {
        'x': nrm(ks[0], (BATCH, SEQ, d), 1.0),
        'c': nrm(ks[1], (BATCH, d), 1.0),
        'ctx': nrm(ks[2], (BATCH, CTX_LEN, d), 1.0),
        'c_ctx': nrm(ks[3], (d,), 1.0),
        'norm_g': 1.0 + nrm(ks[4], (DEPTH_2, d), 0.05),
        'ada_w': nrm(ks[5], (DEPTH_2, d, 3 * d), 0.5 * d ** -0.5),
        'ada_b': nrm(ks[6], (DEPTH_2, 3 * d), 0.02),
        'four_w_in': nrm(ks[7], (N_FOURIER_LAYERS, d, 2 * e), d ** -0.5),
        'four_w_out': nrm(ks[8], (N_FOURIER_LAYERS, e, d), e ** -0.5),
        'attn_w_in': nrm(ks[9], (N_ATTN_LAYERS, d, ATTN_IN), d ** -0.5),
        'attn_sink': nrm(ks[10], (N_ATTN_LAYERS, N_HEADS), 0.5),
        'attn_w_out': nrm(ks[11], (N_ATTN_LAYERS, e, d), e ** -0.5),
        'conv_w_in': nrm(ks[12], (N_CONV_LAYERS, d, 3 * e), d ** -0.5),
        'conv_dw_w': nrm(ks[13], (N_CONV_LAYERS, CONV_WIDTH, e), CONV_WIDTH ** -0.5),
        'conv_dw_b': nrm(ks[14], (N_CONV_LAYERS, e), 0.02),
        'conv_ln_g': 1.0 + nrm(ks[15], (N_CONV_LAYERS, e), 0.05),
        'conv_ln_b': nrm(ks[16], (N_CONV_LAYERS, e), 0.02),
        'conv_w_out': nrm(ks[17], (N_CONV_LAYERS, e, d), e ** -0.5),
        'final_g': 1.0 + nrm(ks[18], (d,), 0.05),
    }

def second_block(x, c, ctx, c_ctx, norm_g, ada_w, ada_b, four_w_in, four_w_out,
              attn_w_in, attn_sink, attn_w_out, conv_w_in, conv_dw_w, conv_dw_b,
              conv_ln_g, conv_ln_b, conv_w_out, final_g):
    n_tokens = x.shape[1]
    cos, sin = axial_rope_tables(n_tokens)
    for i in range(DEPTH_2):
        kind, j = i % N_MIXERS, i // N_MIXERS
        with_ctx = i < DEPTH_2 - 1
        shift, scale, gate = ada_modulation(c, ada_w[i], ada_b[i])
        h = rms_norm_2(x, norm_g[i]) * (1.0 + scale[:, None, :]) + shift[:, None, :]
        shift_c, scale_c, gate_c = ada_modulation(c_ctx, ada_w[i], ada_b[i])
        hc = rms_norm_2(ctx, norm_g[i]) * (1.0 + scale_c) + shift_c
        if kind == 0:
            o = fourier_mix(h, four_w_in[j], four_w_out[j])
            oc = fourier_mix(hc, four_w_in[j], four_w_out[j]) if with_ctx else None
        elif kind == 1:
            o, oc = window_attention_mix(h, hc, attn_w_in[j], attn_sink[j], attn_w_out[j],
                                         cos, sin, with_ctx)
        else:
            conv_args = (conv_w_in[j], conv_dw_w[j], conv_dw_b[j], conv_ln_g[j],
                         conv_ln_b[j], conv_w_out[j])
            o = conformer_conv_mix(h, *conv_args)
            oc = conformer_conv_mix(hc, *conv_args) if with_ctx else None
        x = x + gate[:, None, :] * o
        if with_ctx:
            ctx = ctx + gate_c * oc
    return rms_norm_2(x, final_g)


def setup_inputs(seed=0):
    out = dict(first_inputs(seed))
    for name, value in second_inputs(seed + 1).items():
        if name != "x":
            out[name + "_2"] = value
    return out


def reference(
    x, p, positions, w_in, w_uq, w_ukv, w_o, norm_g, q_norm_g, kv_norm_g, lam_q1, lam_k1,
    lam_q2, lam_k2, subln_g, w_ple, w_pg, final_g, c_2, ctx_2, c_ctx_2, norm_g_2, ada_w_2,
    ada_b_2, four_w_in_2, four_w_out_2, attn_w_in_2, attn_sink_2, attn_w_out_2, conv_w_in_2,
    conv_dw_w_2, conv_dw_b_2, conv_ln_g_2, conv_ln_b_2, conv_w_out_2, final_g_2,
):
    x = first_block(
        x, p, positions, w_in, w_uq, w_ukv, w_o, norm_g, q_norm_g, kv_norm_g, lam_q1, lam_k1,
        lam_q2, lam_k2, subln_g, w_ple, w_pg, final_g,
    )
    return second_block(
        x, c_2, ctx_2, c_ctx_2, norm_g_2, ada_w_2, ada_b_2, four_w_in_2, four_w_out_2,
        attn_w_in_2, attn_sink_2, attn_w_out_2, conv_w_in_2, conv_dw_w_2, conv_dw_b_2,
        conv_ln_g_2, conv_ln_b_2, conv_w_out_2, final_g_2,
    )


_drawn_inputs = setup_inputs


def setup_inputs(seed=0):
    import zlib

    import numpy as np

    out = dict(_drawn_inputs(seed))
    spreads = {}
    factors = {'norm_g': 3.255,
     'q_norm_g': 8.0,
     'kv_norm_g': 8.0,
     'lam_q1': 3.559,
     'lam_k1': 4.991,
     'subln_g': 7.793,
     'final_g': 2.754,
     'ctx_2': 4.126,
     'norm_g_2': 3.074,
     'ada_b_2': 2.899,
     'attn_sink_2': 64.0,
     'conv_dw_b_2': 8.0,
     'conv_ln_g_2': 8.0,
     'conv_ln_b_2': 28.793}
    for name, (base, spread) in spreads.items():
        noise = np.random.default_rng([zlib.crc32(name.encode()), seed]).standard_normal(out[name].shape)
        drawn = base * np.exp(spread * noise) if base else spread * noise
        out[name] = __import__('jax').numpy.asarray(drawn.astype(out[name].dtype))
    for name, factor in factors.items():
        out[name] = (out[name] * factor).astype(out[name].dtype)
    return out
```

```python
import math
from contextlib import ExitStack

import numpy as np
import concourse.bass as bass
from concourse import mybir

F32 = mybir.dt.float32
F32R = mybir.dt.float32r
I32 = mybir.dt.int32
ALU = mybir.AluOpType
ACT = mybir.ActivationFunctionType
AX = mybir.AxisListType

P = 128
D = 2048
KT = D // P
T = 256
EPS = 1e-6
NEG = -1e30
TAKEN = -3e38
BLOCK_COLS = 128
SLABS = 4
TOPK = min(256, T // 4)
LAM_INIT = [0.8 - 0.6 * math.exp(-0.3 * i) for i in range(2)]

Z_GATE = 0
Z_QB, Z_KB, Z_QI, Z_KI, Z_QC, Z_KC, Z_CQ, Z_CKV, Z_KR = 16, 21, 26, 30, 31, 36, 41, 44, 46
V_B, V_W, V_C = 0, 640, 648
V_COLS = 1288
AN_QR, AN_KN = 6, 9

K_ID, K_ROT, K_MASK, K_INVF, K_N = 0, 128, 640, 1152, 1155
K2_DFT, K2_AX, K2_MASK, K2_N = 0, 1024, 1536, 2560


def column_fields():
    sizes = [("norm_g", 32), ("q_norm_g", 6), ("kv_norm_g", 4), ("subln_g", 2), ("final_g", 16),
             ("norm_g_2", 64), ("ada_b_2", 192), ("conv_dw_b_2", 16), ("conv_ln_g_2", 16),
             ("conv_ln_b_2", 16), ("final_g_2", 16), ("c_2", 16), ("c_ctx_2", 16),
             ("conv_dw_w_2", 31 * 16)]
    at, out = 0, {}
    for name, n in sizes:
        out[name] = at
        at += n
    return out, at


COL, NCOL = column_fields()


def stream_plan():
    runs = []

    def run(name, kind, weights, first, groups, steps=None, width=2048):
        runs.append(dict(name=name, kind=kind, w=weights, first=first, n=groups,
                         steps=groups if steps is None else steps, width=width))

    ada = [0]

    def fill(groups):
        run(f"ada{ada[0]}", "A", "ada", ada[0], groups, 0)
        ada[0] += groups

    for l in range(2):
        fill(1)
        run(f"in{l}", "T", "win", 12 * l, 12)
        run(f"v{l}", "N", "wv", 3 * l, 3)
        fill(2)
        run(f"up{l}", "S", "wup", l, 1, 6)
        fill(8)
        run(f"ple{l}", "E", "wple", l, 1, 4, 1024)
        run(f"o{l}", "T", "wo", 4 * l, 4)
        run(f"pg{l}", "T", "wpg", 4 * l, 4)
    fill(2)
    for which, j in (("fc", 0), ("fx", 0), ("f3", 1)):
        if which == "f3":
            fill(2)
            run("kc", "T", "wk", 0, 1)
            run("vc", "N", "wvx", 0, 1)
            run("kx", "T", "wk", 0, 1)
            run("vx", "N", "wvx", 0, 1)
            run("qz", "T", "wqz", 0, 8)
            fill(12)
            run("ao", "T", "wao", 0, 4)
            fill(2)
            run("ci", "T", "wci", 0, 12)
            fill(2)
            run("co", "T", "wco", 0, 4)
            fill(48 - ada[0])
        run(which + "i", "T", "wfi", 8 * j, 8)
        run(which + "o", "T", "wfo", 4 * j, 4)
    q = m = a = e = 0
    for r in runs:
        r["q0"], r["m0"], r["a0"], r["e0"] = q, m, a, e
        q += r["n"]
        if r["kind"] == "A":
            a += r["n"]
        else:
            m += r["n"]
        e += r["steps"]
    assert a == 48
    return runs


RUNS = stream_plan()
RUN = {r["name"]: r for r in RUNS}
ADA_RUNS = [r for r in RUNS if r["kind"] == "A"]


MOD_READS = [(2, 24), (3, 38), (4, 48)]


FILLS = ["n0", "p0", "m0", "g0", "n1", "p1", "m1", "g1",
         "nfc", "yfc", "nfx", "yfx", "nkc", "nx1", "ya", "nci", "yco", "nf3", "yf3"]
SPLITS = {n: i for i, n in enumerate(n for n in FILLS if n[0] != "n")}
NORMS = {n: i for i, n in enumerate(["n0", "n1", "fin", "nfc", "nfx", "nkc", "nx1", "nci", "nf3", "end"])}
U_NORMS = {n: i for i, n in enumerate(n for n in FILLS if n[0] == "n")}


def first_units(l):
    return ([("a", h, 0) for h in range(6)] + [("b", h, 0) for h in range(5)]
            + [("c", h, s) for h in range(5) for s in range(2)])


UNITS1 = first_units(0)
N1 = len(UNITS1)
UNITS2 = [("x", h, b) for h in range(32) for b in range(2)]
N2 = len(UNITS2)
HAS_T1 = [not (m == "c" and s == 0) for m, h, s in UNITS1]
NT1 = sum(HAS_T1)


def unit_numbers():
    flags = HAS_T1 + HAS_T1 + [True] * N2
    out, n = [], 0
    for f in flags:
        n += f
        out.append(n)
    return out


TN = unit_numbers()


def build(nc, w, vec, out):
    ctx = ExitStack()
    with ctx:
        base = 16512
        place = {}

        def sb(name, cols, dt=F32, at=None):
            nonlocal base
            if at is None:
                at = base
                base += (cols * 4 + 31) // 32 * 32
            place[name] = at
            return nc.alloc_sbuf_tensor_at(name, [P, cols], dt, offset=at)

        def sem(name):
            return ctx.enter_context(nc.semaphore(name))

        raw_t = sb("raw", SLABS * 2048)
        whi_t = sb("whi", 2 * 2048, F32R)
        wlo_t = sb("wlo", 2 * 2048, F32R)
        h_t = sb("h", KT * T)
        uhi_t = sb("uhi", KT * T, F32R)
        ulo_t = sb("ulo", KT * T, F32R)
        kk = sb("kk", K_N)
        ones = sb("ones", P)
        cols = sb("cols", NCOL)
        sq = sb("sq", 2048)
        sc = sb("sc", 3 * 512)
        pt = sb("pt", 2 * 512)
        mod = sb("mod", 4 * 96)
        gs = sb("gs", 4 * 32)
        lamr = sb("lamr", 2 * 4 * 64)
        sinkr = sb("sinkr", 32)
        sm = sb("sm", 128)
        arena = base

        def tiles(t, n=T):
            return t[:, :].rearrange("p (k n) -> p k n", n=n)

        raw = tiles(raw_t, 2048)
        whi, wlo = tiles(whi_t, 2048), tiles(wlo_t, 2048)
        hh, uhi, ulo = tiles(h_t), tiles(uhi_t), tiles(ulo_t)
        scs, pts = tiles(sc, 512), tiles(pt, 512)
        tt4 = sc[:, 0:1024].rearrange("p (k n) -> p k n", n=T)
        mods = mod[:, :].rearrange("p (l b c) -> p l b c", l=4, c=2)

        zz_t = sb("zz", 48 * T)
        zz = tiles(zz_t)
        vv = sb("vv", 2 * V_COLS)[:, :].rearrange("p (t n) -> p t n", t=2)
        tabs_t = sb("tabs", 6 * T)
        tabs = tiles(tabs_t)
        praw = tiles(sb("praw", 2 * T, at=place["lamr"]))
        an_t = sb("an", 15 * T, at=place["uhi"])
        an = tiles(an_t)
        va_t = sb("va", 2 * 768, at=place["uhi"] + 15 * T * 4)
        va = va_t[:, :].rearrange("p (t n) -> p t n", t=2)
        cqh = tiles(sb("cqh", 5 * T, F32R, at=place["va"] + 2 * 768 * 4))
        cql = tiles(sb("cql", 5 * T, F32R, at=place["cqh"] + 5 * T * 4))
        assert place["cql"] + 5 * T * 4 <= place["uhi"] + 2 * KT * T * 4
        posi = sb("posi", T, I32, at=place["zz"])
        ang = sb("ang", 3 * T, at=place["zz"] + T * 4)
        trn = sb("trn", 3 * T, at=place["ang"] + 3 * T * 4)
        red = sb("red", 3 * T, at=place["trn"] + 3 * T * 4)

        cc_t = sb("cc", KT * T, at=arena)
        cc = tiles(cc_t)
        zf_t = sb("zf", KT * T, at=arena + 16384)
        zf = tiles(zf_t)
        ab = sb("ab", 2 * 1024, at=arena + 32768)[:, :].rearrange("p (s t n) -> p s t n", s=2, t=2)
        zq_t = sb("zq", 32 * T, at=arena)
        zq = tiles(zq_t)
        kx = tiles(sb("kx", 4 * T, at=arena + 32768))
        kc = tiles(sb("kc", 4 * T, at=arena + 36864))
        vx = tiles(sb("vx", 2 * T, at=arena + 40960))
        vc = tiles(sb("vc", 2 * T, at=arena + 43008))
        PADT = T + 30
        gp_t = sb("gp", KT * PADT, at=arena)
        gp = gp_t[:, :].rearrange("p (k n) -> p k n", n=PADT)
        zs_t = sb("zs", KT * T, at=arena + KT * PADT * 4)
        zs = tiles(zs_t)
        yc_t = sb("yc", KT * T, at=arena + KT * PADT * 4 + 16384)
        yc = tiles(yc_t)
        k2 = sb("k2", K2_N, at=arena + 52224)
        assert arena + 52224 + K2_N * 4 <= 229368 and base <= 229368, (base, arena)
        dft = k2[:, K2_DFT:K2_DFT + 1024].rearrange("p (k n) -> p k n", k=2)

        bank = [ctx.enter_context(nc.psum_tensor(f"bank{i}", [P, 512], F32)) for i in range(8)]

        ident = kk[:, K_ID:K_ID + P]
        mask1 = kk[:, K_MASK:K_MASK + 512]
        mask2 = k2[:, K2_MASK:K2_MASK + 1024].rearrange("p (b n) -> p b n", b=2)

        def rot(i):
            return kk[:, K_ROT + P * i:K_ROT + P * (i + 1)]

        def col(name, i, n=1):
            return cols[:, COL[name] + i:COL[name] + i + n]

        s_in = sem("inputs_loaded")
        s_p = sem("ple_input_loaded")
        s_c = sem("context_loaded")
        s_const = sem("constants_set")
        s_raw = [sem(f"slab_loaded{i}") for i in range(SLABS)]
        s_hi = sem("slab_hi_ready")
        s_lo = sem("slab_lo_ready")
        s_slab = sem("slab_multiplied")
        s_ada = sem("ada_slab_multiplied")
        s_up = sem("lowrank_blocks_summed")
        s_drain = sem("projection_drained")
        s_gu = sem("gate_used")
        s_uh = sem("u_hi_ready")
        s_ul = sem("u_lo_ready")
        s_sq = sem("squares_ready")
        s_ss = sem("squares_summed")
        s_rt = sem("root_ready")
        s_nt = sem("normed_ready")
        s_nh = sem("normed_hi_ready")
        s_nl = sem("normed_lo_ready")
        s_csq = sem("lowrank_squares_ready")
        s_css = sem("lowrank_squares_summed")
        s_crt = sem("lowrank_root_ready")
        s_ct = sem("lowrank_normed_ready")
        s_ch = sem("lowrank_hi_ready")
        s_cl = sem("lowrank_lo_ready")
        s_rm = sem("rope_rotated")
        s_ro = sem("rope_done")
        s_gate = sem("gates_ready")
        s_im = sem("index_scores_ready")
        s_ir = sem("index_relu_ready")
        s_ia = sem("index_added")
        s_s = sem("scores_ready")
        s_sd = sem("scores_drained")
        s_m = sem("max_ready")
        s_e = sem("exp_ready")
        s_pr = sem("probs_ready")
        s_t = sem("probs_transposed")
        s_tc = sem("probs_copied")
        s_o = sem("heads_out_ready")
        s_of = sem("heads_out_used")
        s_osq = sem("subln_squares_ready")
        s_oss = sem("subln_squares_summed")
        s_ort = sem("subln_root_ready")
        s_mix = sem("mixed_ready")
        s_lam = sem("lambda_steps")
        s_sin = sem("table_angle_ready")
        s_tab = sem("tables_ready")
        s_mod = sem("modulation_ready")
        s_sil = sem("cond_silu_ready")
        s_f1 = sem("dft_tokens_ready")
        s_fa = sem("dft_tokens_copied")
        s_f2 = sem("dft_summed")
        s_fb = sem("dft_copied")
        s_cg = sem("conv_gates_ready")
        s_conv = sem("conv_done")
        s_lnq = sem("conv_squares_ready")
        s_lns = sem("conv_sums_ready")
        s_lnr = sem("conv_root_ready")
        s_lny = sem("conv_normed_ready")
        s_lnz = sem("conv_silu_ready")
        s_yd = sem("gated_ready")
        s_rt2 = sem("conv_root_ready_root")
        s_yc = sem("conv_gated_ready")
        s_fin = sem("first_block_normed")
        s_out = sem("output_stored")
        s_dv = sem("vector_steps")
        s_ac = sem("scalar_steps")

        INPUT_DMAS = 7

        def slab_loads(r, g, s):
            return (r["q0"] + g + 1) * 16

        def rope_jobs():
            jobs = [(zz_t[:, T * b:T * (b + 2)], 1, 2) for b in range(Z_QB, Z_QB + 10, 2)]
            jobs += [(zz_t[:, T * b:T * min(b + 2, Z_QI + 15)], 2, min(2, Z_QI + 15 - b))
                     for b in range(Z_QI, Z_QI + 15, 2)]
            jobs += [(zz_t[:, T * Z_KR:T * (Z_KR + 1)], 0, 1)]
            jobs += [(an_t[:, T * 6:T * 8], 0, 2), (an_t[:, T * 8:T * 9], 0, 1)]
            return jobs

        NJ = 16
        NJX = 10

        def rope_jobs_x():
            jobs = [(kx[:, 2 * i:2 * i + 2, :].rearrange("p k n -> p (k n)"), 3, 2) for i in range(2)]
            return jobs + [(zq_t[:, T * 2 * i:T * 2 * (i + 1)], 3, 2) for i in range(8)]

        block = ctx.enter_context(nc.Block())

        @block.sync
        def _(sp):
            def load(r, g, s):
                src = w[r["w"]]
                if r["width"] == 2048:
                    sp.dma_start(raw[:, s, :], src[r["first"] + g, s]).then_inc(s_raw[s], 16)
                else:
                    sp.dma_start(raw[:, s, 0:r["width"]],
                                 src[r["first"] + g, s, :, 0:r["width"]]).then_inc(s_raw[s], 16)

            before = None
            for r in RUNS:
                for s in range(SLABS):
                    if before is not None and before["kind"] == "A":
                        sp.wait_ge(s_ada, SLABS * (before["a0"] + before["n"] - 1) + s + 1)
                    elif before is not None:
                        sp.wait_ge(s_lo, SLABS * (before["m0"] + before["n"] - 1) + s + 1)
                    load(r, 0, s)
                if r["n"] > 1:
                    with sp.Fori(1, r["n"]) as g:
                        for s in range(SLABS):
                            if r["kind"] == "A":
                                sp.wait_ge(s_ada, g * SLABS + (SLABS * (r["a0"] - 1) + s + 1)
                                           if r["a0"] else g * SLABS + (s + 1) - SLABS)
                            else:
                                sp.wait_ge(s_lo, g * SLABS + (SLABS * (r["m0"] - 1) + s + 1)
                                           if r["m0"] else g * SLABS + (s + 1) - SLABS)
                            load(r, g, s)
                before = r
            for c in range(4):
                sp.wait_ge(s_yd, c + 1)
                sp.dma_start(out[:, 4 * c:4 * c + 4, :], zf[:, 4 * c:4 * c + 4, :]).then_inc(s_out, 16)
            sp.wait_ge(s_out, 64)

        @block.gpsimd
        def _(pool):
            nc.gpsimd.memset(ones[:, :], 1.0).then_inc(s_const, 1)
            pool.wait_ge(s_lam, 1)
            pool.dma_start(praw[:, :, :], vec["p"][0]).then_inc(s_p, 16)
            pool.wait_ge(s_ul, 4 * SPLITS["p0"] + 4)
            pool.dma_start(praw[:, :, :], vec["p"][1]).then_inc(s_p, 16)
            pool.wait_ge(s_gu, 8)
            pool.dma_start(cc[:, :, :], vec["ctx"]).then_inc(s_c, 16)
            pool.dma_start(k2[:, :], vec["consts2"]).then_inc(s_c, 16)

        @block.tensor
        def _(pe):
            ada_at = [0]

            def filled(fill, s):
                if fill in NORMS:
                    return s_nl, 16 * U_NORMS[fill] + 4 * (s + 1)
                return s_ul, 4 * SPLITS[fill] + s + 1

            def mm3(o, whi_, wlo_, xhi_, xlo_, start, stop):
                nc.tensor.matmul(o, whi_, xhi_, start=start, stop=False, skip_group_check=True)
                nc.tensor.matmul(o, whi_, xlo_, start=False, stop=False, skip_group_check=True)
                return nc.tensor.matmul(o, wlo_, xhi_, start=False, stop=stop, skip_group_check=True)

            def step_banks(e):
                return (bank[2 * (e % 2)], bank[2 * (e % 2) + 1])

            def slab_t(s, par):
                for k in range(4):
                    kt = 4 * s + k
                    for b in range(4):
                        wc = slice(512 * k + P * b, 512 * k + P * (b + 1))
                        o = bank[2 * par + b // 2][:, T * (b % 2):T * (b % 2) + T]
                        last = mm3(o, whi[:, s % 2, wc], wlo[:, s % 2, wc], uhi[:, kt, :], ulo[:, kt, :],
                                   kt == 0 and b % 2 == 0, kt == KT - 1)
                return last

            def slab_n(s, par, width):
                for k in range(4):
                    kt = 4 * s + k
                    for t in range(2):
                        tk = slice(P * t, P * (t + 1))
                        wc = slice(512 * k, 512 * k + width)
                        o = bank[2 * par + t][:, 0:width]
                        nc.tensor.matmul(o, uhi[:, kt, tk], whi[:, s % 2, wc], start=kt == 0,
                                         stop=False, skip_group_check=True)
                        nc.tensor.matmul(o, uhi[:, kt, tk], wlo[:, s % 2, wc], start=False,
                                         stop=False, skip_group_check=True)
                        last = nc.tensor.matmul(o, ulo[:, kt, tk], whi[:, s % 2, wc], start=False,
                                                stop=kt == KT - 1, skip_group_check=True)
                return last

            def group(r, g, par, slab, fill=None):
                e = g + r["e0"]
                if not (isinstance(e, int) and e < 2):
                    pe.wait_ge(s_drain, (e - 1) * 2)
                for s in range(SLABS):
                    if fill is not None:
                        pe.wait_ge(*filled(fill, s))
                    pe.wait_ge(s_lo, (g + r["m0"]) * SLABS + (s + 1))
                    last = slab(s, par)
                    last.then_inc(s_slab, 1)

            def project(name, fill, width=512):
                r = RUN[name]
                n, e0 = r["n"], r["e0"]
                slab = slab_t if r["kind"] == "T" else (lambda s, par: slab_n(s, par, width))
                group(r, 0, e0 % 2, slab, fill)
                if n == 1:
                    return
                group(r, 1, (e0 + 1) % 2, slab)
                if n == 2:
                    return
                with pe.Fori(1, n // 2) as j:
                    for half in range(2):
                        group(r, j * 2 + half, (e0 + half) % 2, slab)

            def ada(groups):
                for _ in range(groups):
                    a = ada_at[0]
                    ada_at[0] += 1
                    q = next(r["q0"] + a - r["a0"] for r in ADA_RUNS if r["a0"] <= a < r["a0"] + r["n"])
                    layer, g = a // 12, a % 12
                    at = 96 * layer + 8 * g
                    if a == 0:
                        pe.wait_ge(s_sil, 1)
                    for mods_read, groups in MOD_READS:
                        if a == groups:
                            pe.wait_ge(s_mod, mods_read)
                    for s in range(SLABS):
                        pe.wait_ge(s_raw[s], 16 * (q + 1))
                        for k in range(4):
                            kt = 4 * s + k
                            for b in range(4):
                                last = nc.tensor.matmul(
                                    bank[4][:, at + 2 * b:at + 2 * b + 2],
                                    raw[:, s, 512 * k + P * b:512 * k + P * (b + 1)],
                                    sm[:, 32 + 2 * kt:34 + 2 * kt],
                                    start=a == 0 and kt == 0 and b == 0, stop=kt == KT - 1,
                                    skip_group_check=True)
                        last.then_inc(s_ada, 1)

            def norm(name):
                n = NORMS[name]
                for c in range(4):
                    pe.wait_ge(s_sq, 4 * n + c + 1)
                    for k in range(4):
                        last = nc.tensor.matmul(bank[7][:, 0:T], ones[:, :],
                                                sq[:, 1024 * (c % 2) + T * k:1024 * (c % 2) + T * (k + 1)],
                                                start=c == 0 and k == 0, stop=c == 3 and k == 3)
                    last.then_inc(s_ss, 1)

            def ropes(jobs, base_job, ready):
                for i, (x, kind, nb) in enumerate(jobs):
                    ready(i)
                    j = base_job + i
                    if i >= 2:
                        pe.wait_ge(s_ro, j - 1)
                    nc.tensor.matmul(bank[5 + i % 2][:, 0:T * nb], rot(kind), x,
                                     start=True, stop=True).then_inc(s_rm, 1)

            def softmax_units(first, n, scores, transposes, values, busy):
                for t in range(n + 3):
                    if t < n:
                        u = first + t
                        if t >= 2:
                            pe.wait_ge(s_sd, u - 1)
                        scores(t, bank[t % 2]).then_inc(s_s, 1)
                    if 2 <= t < n + 2:
                        i = t - 2
                        tn = TN[first + i]
                        if transposes(i, None, None):
                            pe.wait_ge(s_pr, first + i + 1)
                            if i >= 2:
                                pe.wait_ge(s_tc, tn - 2)
                            transposes(i, bank[2 + tn % 2], scs[:, i % 3, :]).then_inc(s_t, 1)
                    if t >= 3:
                        i = t - 3
                        tn = TN[first + i]
                        if transposes(i, None, None):
                            pe.wait_ge(s_tc, tn)
                            values(i, pts[:, tn % 2, :]).then_inc(s_o, 1)
                    busy(t)

            def first_block(l):
                norm(f"n{l}")
                ada(1)
                project(f"in{l}", f"n{l}")
                r = RUN[f"v{l}"]
                for g in range(3):
                    group(r, g, (r["e0"] + g) % 2,
                          lambda s, par, n=512 if g < 2 else V_COLS - 1024: slab_n(s, par, n))
                jobs = rope_jobs()
                pe.wait_ge(s_drain, 2 * (RUN[f"v{l}"]["e0"] + 3))
                pe.wait_ge(s_csq, l + 1)
                for k in range(5):
                    last = nc.tensor.matmul(bank[7][:, T * (k > 2):T * (k > 2) + T], ones[:, :],
                                            sq[:, T * k:T * (k + 1)], start=k in (0, 3), stop=k in (2, 4),
                                            skip_group_check=True)
                last.then_inc(s_css, 1)
                ropes(jobs[:14], NJ * l, lambda i: None)
                ada(2)
                up(l)
                pe.wait_ge(s_drain, 2 * (RUN[f"up{l}"]["e0"] + 6))
                for i, (x, kind, nb) in enumerate(jobs[14:]):
                    pe.wait_ge(s_ro, NJ * l + 14 + i - 1)
                    nc.tensor.matmul(bank[5 + i % 2][:, 0:T * nb], rot(kind), x,
                                     start=True, stop=True).then_inc(s_rm, 1)
                pe.wait_ge(s_ro, NJ * l + 16)
                for h in range(8):
                    if h >= 2:
                        pe.wait_ge(s_ir, 8 * l + h - 1)
                    rows = slice(64 * (h % 2), 64 * (h % 2) + 64)
                    for t in range(2):
                        last = nc.tensor.matmul(bank[5 + h % 2][:, T * t:T * (t + 1)],
                                                zz[rows, Z_QI + h // 2, P * t:P * (t + 1)],
                                                zz[rows, Z_KI, :], start=True, stop=True,
                                                skip_group_check=True)
                    last.then_inc(s_im, 1)

                def scores(i, ps):
                    m, h, part = UNITS1[i]
                    for t in range(2):
                        o = ps[:, T * t:T * (t + 1)]
                        tk = slice(P * t, P * (t + 1))
                        if m == "a":
                            rows = slice(64 * (h % 2), 64 * (h % 2) + 64)
                            nc.tensor.matmul(o, an[:, h, tk], an[:, AN_KN + h, :], start=True,
                                             stop=False, skip_group_check=True)
                            last = nc.tensor.matmul(o, an[rows, AN_QR + h // 2, tk], zz[rows, Z_KR, :],
                                                    start=False, stop=True, skip_group_check=True)
                        elif m == "b":
                            last = nc.tensor.matmul(o, zz[:, Z_QB + h, tk], zz[:, Z_KB + h, :],
                                                    start=True, stop=True, skip_group_check=True)
                        else:
                            rows = slice(64 * part, 64 * part + 64)
                            last = nc.tensor.matmul(o, zz[rows, Z_QC + h, tk], zz[rows, Z_KC + h, :],
                                                    start=True, stop=True, skip_group_check=True)
                    return last

                def transposes(i, ps, pr):
                    if ps is None:
                        return HAS_T1[i]
                    for n, c in enumerate((0, 2, 3)):
                        last = nc.tensor.transpose(ps[:, P * n:P * (n + 1)], pr[:, P * c:P * (c + 1)], ident)
                    return last

                def values(i, p):
                    m, h, part = UNITS1[i]
                    tn = TN[N1 * l + i] - 1
                    if tn % NT1 >= 2 or True:
                        if tn >= 2:
                            pe.wait_ge(s_of, tn - 1)
                    o = bank[5 + tn % 2]
                    if m == "a":
                        v = [va[:, k, P * h:P * (h + 1)] for k in range(2)]
                    else:
                        at = (V_B if m == "b" else V_C) + P * h
                        v = [vv[:, k, at:at + P] for k in range(2)]
                    nc.tensor.matmul(o[:, 0:P], v[0], p[:, 0:P], start=True, stop=True,
                                     skip_group_check=True)
                    nc.tensor.matmul(o[:, P:T], v[0], p[:, P:2 * P], start=True, stop=False,
                                     skip_group_check=True)
                    return nc.tensor.matmul(o[:, P:T], v[1], p[:, 2 * P:3 * P], start=False, stop=True,
                                            skip_group_check=True)

                pe.wait_ge(s_ir, 8 * l + 8)
                fill = [8]

                def busy(t):
                    if fill[0] and t % 3 == 1:
                        ada(1)
                        fill[0] -= 1
                softmax_units(N1 * l, N1, scores, transposes, values, busy)
                while fill[0]:
                    busy(1)
                pe.wait_ge(s_osq, l + 1)
                for c in range(3):
                    n = 512 if c < 2 else 256
                    last = nc.tensor.matmul(bank[5 + c][:, 0:n], ones[:, :], sq[:, 512 * c:512 * c + n],
                                            start=True, stop=True)
                last.then_inc(s_oss, 1)
                r = RUN[f"ple{l}"]
                pe.wait_ge(s_ul, 4 * SPLITS[f"p{l}"] + 4)
                for s in range(SLABS):
                    pe.wait_ge(s_drain, 2 * (r["e0"] + s - 1))
                    pe.wait_ge(s_lo, SLABS * r["m0"] + s + 1)
                    b0, b1 = step_banks(r["e0"] + s)
                    for k in range(2):
                        for b in range(4):
                            wc = slice(512 * k + P * b, 512 * k + P * (b + 1))
                            o = (b0, b1)[b // 2][:, T * (b % 2):T * (b % 2) + T]
                            last = mm3(o, whi[:, s % 2, wc], wlo[:, s % 2, wc], uhi[:, k, :], ulo[:, k, :],
                                       k == 0 and b % 2 == 0, k == 1)
                    last.then_inc(s_slab, 1)
                project(f"o{l}", f"m{l}")
                project(f"pg{l}", f"g{l}")

            def up(l):
                r = RUN[f"up{l}"]
                pe.wait_ge(s_cl, l + 1)
                slab = [-1]

                def need(s):
                    if s > slab[0]:
                        pe.wait_ge(s_lo, SLABS * r["m0"] + s + 1)
                        slab[0] = s

                tile = 0
                for b in range(15):
                    e = r["e0"] + b // 4
                    o = step_banks(e)[(b % 4) // 2][:, T * (b % 2):T * (b % 2) + T]
                    if b % 4 == 0:
                        pe.wait_ge(s_drain, 2 * (e - 1))
                    nk, k0 = (3, 0) if b < 9 else (2, 3)
                    if b == 5:
                        tile = 16
                    for k in range(nk):
                        s = tile // 16
                        need(s)
                        wc = slice(P * (tile % 16), P * (tile % 16 + 1))
                        last = mm3(o, whi[:, s % 2, wc], wlo[:, s % 2, wc], cqh[:, k0 + k, :],
                                   cql[:, k0 + k, :], k == 0 and b % 2 == 0, k == nk - 1)
                        tile += 1
                    if b in (4, 10):
                        last.then_inc(s_slab, 1)
                    if b in (3, 7, 11, 14):
                        last.then_inc(s_up, 1)
                for part, (s, c0, n) in enumerate(((2, 1024, 512), (3, 0, 256))):
                    e = r["e0"] + 4 + part
                    pe.wait_ge(s_drain, 2 * (e - 1))
                    need(s)
                    for t in range(2):
                        tk = slice(P * t, P * (t + 1))
                        o = step_banks(e)[t][:, 0:n]
                        for k in range(2):
                            wc = slice(c0 + n * k, c0 + n * (k + 1))
                            nc.tensor.matmul(o, cqh[:, 3 + k, tk], whi[:, s % 2, wc], start=k == 0,
                                             stop=False, skip_group_check=True)
                            nc.tensor.matmul(o, cqh[:, 3 + k, tk], wlo[:, s % 2, wc], start=False,
                                             stop=False, skip_group_check=True)
                            last = nc.tensor.matmul(o, cql[:, 3 + k, tk], whi[:, s % 2, wc], start=False,
                                                    stop=k == 1, skip_group_check=True)
                    last.then_inc(s_slab, 1)

            def fourier(tag, n_inv, fill):
                norm("nf" + tag)
                ada(fill)
                r = RUN[f"f{tag}i"]
                project_part(r, 0, 4, f"nf{tag}")
                for g in range(8):
                    for t in range(2):
                        if g == 0 and t == 0:
                            pe.wait_ge(s_drain, 2 * (r["e0"] + 4))
                        i = 16 * n_inv + 2 * g + t
                        if i >= 2:
                            pe.wait_ge(s_fa, i - 1)
                        for k in range(2):
                            last = nc.tensor.matmul(bank[5 + t][:, :], zf[:, 2 * g + k, P * t:P * (t + 1)],
                                                    dft[:, k, :], start=k == 0, stop=k == 1)
                        last.then_inc(s_f1, 1)
                    pe.wait_ge(s_fa, 16 * n_inv + 2 * g + 2)
                    if 8 * n_inv + g >= 1:
                        pe.wait_ge(s_fb, 8 * n_inv + g)
                    for b in range(2):
                        n = 0
                        for cs in range(2):
                            for k in range(2):
                                last = nc.tensor.matmul(bank[7][:, T * b:T * (b + 1)],
                                                        ab[:, g % 2, k, T * cs + P * b:T * cs + P * (b + 1)],
                                                        dft[:, k, T * cs:T * (cs + 1)],
                                                        start=n == 0, stop=n == 3, skip_group_check=True)
                                n += 1
                    last.then_inc(s_f2, 1)
                project_part(r, 4, 4, None)
                project(f"f{tag}o", f"yf{tag}")

            def project_part(r, g0, n, fill):
                for g in range(g0, g0 + 1):
                    group(r, g, (r["e0"] + g) % 2, slab_t, fill)
                group(r, g0 + 1, (r["e0"] + g0 + 1) % 2, slab_t)
                with pe.Fori(g0 // 2 + 1, (g0 + n) // 2) as j:
                    for half in range(2):
                        group(r, j * 2 + half, (r["e0"] + half) % 2, slab_t)

            pe.wait_ge(s_const, 1)
            pe.wait_ge(s_in, 16 * INPUT_DMAS)
            for l in range(2):
                first_block(l)
            norm("fin")
            pe.wait_ge(s_c, 32)
            fourier("c", 0, 2)
            fourier("x", 1, 0)
            norm("nkc")
            ada(2)
            project("kc", "nkc")
            project("vc", None, 256)
            norm("nx1")
            project("kx", "nx1")
            project("vx", None, 256)
            project("qz", None)
            pe.wait_ge(s_drain, 2 * (RUN["qz"]["e0"] + 8))
            ropes(rope_jobs_x(), 2 * NJ, lambda i: None)
            pe.wait_ge(s_ro, 2 * NJ + NJX)

            def scores(i, ps):
                _, h, b = UNITS2[i]
                rows = slice(64 * (h % 2), 64 * (h % 2) + 64)
                q = zq[rows, h // 2, P * b:P * (b + 1)]
                nc.tensor.matmul(ps[:, 0:T], q, kx[rows, h // 8, :], start=True, stop=True,
                                 skip_group_check=True)
                return nc.tensor.matmul(ps[:, T:2 * T], q, kc[rows, h // 8, :], start=True, stop=True,
                                        skip_group_check=True)

            def transposes(i, ps, pr):
                if ps is None:
                    return True
                for c in range(4):
                    last = nc.tensor.transpose(ps[:, P * c:P * (c + 1)], pr[:, P * c:P * (c + 1)], ident)
                return last

            def values(i, p):
                _, h, b = UNITS2[i]
                if h % 2 == 0 and b == 0:
                    pe.wait_ge(s_of, 2 * NT1 + max(0, h // 2 - 1))
                o = bank[5 + (h // 2) % 2][64 * (h % 2):64 * (h % 2) + 64, P * b:P * (b + 1)]
                for c in range(4):
                    v = (vx if c < 2 else vc)[:, c % 2, 64 * (h // 8):64 * (h // 8) + 64]
                    last = nc.tensor.matmul(o, v, p[:, P * c:P * (c + 1)], start=c == 0, stop=c == 3,
                                            skip_group_check=True)
                return last

            fill = [12]

            def busy(t):
                if fill[0] and t % 5 == 1:
                    ada(1)
                    fill[0] -= 1
            softmax_units(2 * N1, N2, scores, transposes, values, busy)
            project("ao", "ya")
            norm("nci")
            ada(2)
            project("ci", "nci")
            for c in range(4):
                pe.wait_ge(s_conv, 4 * c + 4)
                for k in range(4):
                    last = nc.tensor.matmul(bank[5][:, 0:T], ones[:, :], yc[:, 4 * c + k, :],
                                            start=c == 0 and k == 0, stop=c == 3 and k == 3)
            last.then_inc(s_lns, 1)
            for c in range(4):
                pe.wait_ge(s_lnq, c + 1)
                for k in range(4):
                    last = nc.tensor.matmul(bank[6][:, 0:T], ones[:, :],
                                            sq[:, 1024 * (c % 2) + T * k:1024 * (c % 2) + T * (k + 1)],
                                            start=c == 0 and k == 0, stop=c == 3 and k == 3)
                last.then_inc(s_lns, 1)
            ada(2)
            project("co", "yco")
            fourier("3", 2, 48 - ada_at[0])
            norm("end")

        def residual(name):
            if name.startswith("pg"):
                return s_gu, 4 * (int(name[2]) + 1)
            r = RUN[name]
            return s_drain, 2 * (r["e0"] + r["n"])

        NORM_ARGS = {
            "n0": (hh, "in", None), "n1": (hh, "pg0", None), "nfc": (cc, "c", (0, 1)),
            "fin": (hh, "pg1", None), "nfx": (hh, "fin", (0, 0)), "nkc": (cc, "fco", (1, 1)), "nx1": (hh, "fxo", (1, 0)),
            "nci": (hh, "ao", (2, 0)), "nf3": (hh, "co", (3, 0)), "end": (hh, "f3o", None),
        }
        GATED = {"pg0": 0, "pg1": 4, "fc": 8, "fx": 12, "f3": 16}
        SM_NM, SM_SUM, SM_RI, SM_RL, SM_SIL, SM_LAM, SM_SUBG, SM_TMP, SM_M8, SM_ES = (
            0, 8, 16, 24, 32, 64, 66, 68, 80, 96)

        def source_ready(eng, name):
            src = NORM_ARGS[name][1]
            if src == "in":
                eng.wait_ge(s_in, 16 * INPUT_DMAS)
            elif src == "c":
                eng.wait_ge(s_c, 32)
            elif src == "fin":
                eng.wait_ge(s_fin, 1)
            else:
                eng.wait_ge(*residual(src))

        def norm_scale(name, kt):
            if name in ("n0", "n1"):
                return col("norm_g", 16 * int(name[1]) + kt)
            if name == "end":
                return col("final_g_2", kt)
            if name == "fin":
                return col("final_g", kt)
            l, c = NORM_ARGS[name][2]
            return gs[:, 32 * l + 16 * c + kt:32 * l + 16 * c + kt + 1]

        def norm_shift(name, kt):
            if NORM_ARGS[name][2] is None:
                return None
            l, c = NORM_ARGS[name][2]
            return mods[:, l, kt, c:c + 1]

        @block.scalar
        def _(act):
            steps = [0]

            def link(ins):
                steps[0] += 1
                ins.then_inc(s_ac, 1)
                act.wait_ge(s_ac, steps[0])

            def split(r, g, s):
                act.wait_ge(s_raw[s], (g + (r["q0"] + 1)) * 16)
                n = r["width"]
                m = g * SLABS + (SLABS * r["m0"] + s)
                if not (isinstance(m, int) and m < 2):
                    act.wait_ge(s_slab, m - 1)
                nc.scalar.copy(whi[:, s % 2, 0:n], raw[:, s, 0:n]).then_inc(s_hi, 1)

            def presplit(name, g=0):
                split(RUN[name], g, 0)
                split(RUN[name], g, 1)

            def summed(r, g):
                act.wait_ge(s_slab, (g + (r["m0"] + 1)) * SLABS)

            def run(r, drain, g0=0, n=None, pre=True, then=None):
                n = r["n"] if n is None else n
                if not pre:
                    split(r, g0, 0)
                    split(r, g0, 1)
                split(r, g0, 2)
                split(r, g0, 3)

                def body(g, par):
                    split(r, g, 0)
                    split(r, g, 1)
                    drain(r, g - 1, par)
                    split(r, g, 2)
                    split(r, g, 3)
                pairs = (n - 1) // 2
                if pairs > 1:
                    with act.Fori(0, pairs) as j:
                        for half in range(2):
                            body(j * 2 + (g0 + 1 + half), (r["e0"] + g0 + half) % 2)
                else:
                    for g in range(1, 1 + 2 * pairs):
                        body(g0 + g, (r["e0"] + g0 + g - 1) % 2)
                if (n - 1) % 2:
                    body(g0 + n - 1, (r["e0"] + g0 + n - 2) % 2)
                if then is not None:
                    presplit(*then)
                drain(r, g0 + n - 1, (r["e0"] + g0 + n - 1) % 2)

            def nothing(r, g, par):
                pass

            def copier(dest, func=ACT.Copy):
                def drain(r, g, par):
                    summed(r, g)
                    for half in range(2):
                        last = nc.scalar.activation(dest(g, half), bank[2 * par + half][:, :], func)
                    last.then_inc(s_drain, 2)
                return drain

            def gater(first, func, g0):
                def drain(r, g, par):
                    i = first + g - g0
                    if i >= 2:
                        act.wait_ge(s_gu, i - 1)
                    summed(r, g)
                    for half in range(2):
                        at = 1024 * (i % 2) + 512 * half
                        last = nc.scalar.activation(sq[:, at:at + 512], bank[2 * par + half][:, :], func)
                    last.then_inc(s_drain, 2)
                return drain

            def norm(name):
                n = NORMS[name]
                src = NORM_ARGS[name][0]
                source_ready(act, name)
                for c in range(4):
                    if 4 * n + c >= 2:
                        act.wait_ge(s_ss, 4 * n + c - 1)
                    nc.scalar.activation(sq[:, 1024 * (c % 2):1024 * (c % 2 + 1)],
                                         src[:, 4 * c:4 * c + 4, :].rearrange("p k n -> p (k n)"),
                                         ACT.Square).then_inc(s_sq, 1)
                act.wait_ge(s_ss, 4 * n + 4)
                if name == "nfc":
                    act.wait_ge(s_fin, 1)
                nc.scalar.activation(sc[:, 1024:1024 + T], bank[7][:, 0:T], ACT.Sqrt, bias=EPSB,
                                     scale=1.0 / D).then_inc(s_rt, 1)
                if name in ("fin", "end"):
                    return
                for kt in range(KT):
                    act.wait_ge(s_nt, 16 * U_NORMS[name] + kt + 1)
                    sh = norm_shift(name, kt)
                    if sh is None:
                        nc.scalar.copy(uhi[:, kt, :], tt4[:, kt % 4, :]).then_inc(s_nh, 1)
                    else:
                        nc.scalar.activation(uhi[:, kt, :], tt4[:, kt % 4, :], ACT.Identity,
                                             bias=sh).then_inc(s_nh, 1)

            def fill_u(name, src, next_run, chunks=4, width=1024):
                act.wait_ge(s_slab, SLABS * RUN[next_run]["m0"])
                for c in range(chunks):
                    nc.scalar.copy(uhi_t[:, width * c:width * (c + 1)],
                                   src[:, width * c:width * (c + 1)]).then_inc(s_uh, 1)

            EPSB = sm[:, 100:101]

            def softmax_units(first, n, exps, transposed):
                for t in range(n + 2):
                    if t < n:
                        u = first + t
                        act.wait_ge(s_m, u + 1)
                        exps(t).then_inc(s_e, 1)
                    if t >= 2:
                        i = t - 2
                        if not transposed(i):
                            continue
                        tn = TN[first + i]
                        act.wait_ge(s_t, tn)
                        if tn > 2:
                            act.wait_ge(s_o, tn - 2)
                        width = 3 * P if first < 2 * N1 else 4 * P
                        nc.scalar.copy(pts[:, tn % 2, 0:width], bank[2 + tn % 2][:, 0:width])\
                            .then_inc(s_tc, 1)

            for dst, src in ((hh, vec["x"]),):
                act.dma_start(dst[:, :, :], src).then_inc(s_in, 16)
            act.dma_start(kk[:, :], vec["consts"]).then_inc(s_in, 16)
            act.dma_start(cols[:, :], vec["cols"]).then_inc(s_in, 16)
            act.dma_start(lamr[:, :], vec["lam"]).then_inc(s_in, 16)
            act.dma_start(sinkr[:, :], vec["sink"]).then_inc(s_in, 16)
            act.dma_start(posi[:, :], vec["pos"]).then_inc(s_in, 16)
            act.dma_start(sm[:, 100:101], vec["eps"]).then_inc(s_in, 16)
            act.wait_ge(s_in, 16 * INPUT_DMAS)
            nc.scalar.activation(sm[:, SM_SIL:SM_SIL + 32:2], col("c_2", 0, 16), ACT.Silu)
            nc.scalar.activation(sm[:, SM_SIL + 1:SM_SIL + 32:2], col("c_ctx_2", 0, 16), ACT.Silu)\
                .then_inc(s_sil, 1)
            act.wait_ge(s_lam, 1)
            nc.scalar.activation(sm[:, SM_TMP + 4:SM_TMP + 8], sm[:, SM_TMP:SM_TMP + 4], ACT.Exp)\
                .then_inc(s_lam, 1)
            for i in range(2):
                act.wait_ge(s_sin, i + 1)
                nc.scalar.activation(tabs[:, i::2, :], red[:, :].rearrange("p (k n) -> p k n", n=T),
                                     ACT.Sin).then_inc(s_tab, 1)

            def first_block(l):
                norm(f"n{l}")
                run(RUN[f"in{l}"], copier(lambda g, half: zz_t[:, bass.ds(g * 1024 + 512 * half, 512)]
                                          if not isinstance(g, int) else
                                          zz_t[:, 1024 * g + 512 * half:1024 * g + 512 * half + 512]),
                    pre=False, then=(f"v{l}",))

                def drain_v(r, g, par):
                    summed(r, g)
                    n = 512 if g < 2 else V_COLS - 1024
                    for t in range(2):
                        last = nc.scalar.copy(vv[:, t, 512 * g:512 * g + n], bank[2 * par + t][:, 0:n])
                    last.then_inc(s_drain, 2)
                run(RUN[f"v{l}"], drain_v)
                act.wait_ge(s_drain, 2 * (RUN[f"v{l}"]["e0"] + 3))
                nc.scalar.activation(sq[:, 0:5 * T], zz_t[:, T * Z_CQ:T * (Z_CQ + 5)], ACT.Square)\
                    .then_inc(s_csq, 1)
                act.wait_ge(s_css, l + 1)
                nc.scalar.activation(sc[:, 0:T], bank[7][:, 0:T], ACT.Sqrt, bias=EPSB, scale=1.0 / 384)
                nc.scalar.activation(sc[:, T:2 * T], bank[7][:, T:2 * T], ACT.Sqrt, bias=EPSB,
                                     scale=1.0 / 256).then_inc(s_crt, 1)
                nc.scalar.activation(zz_t[:, 0:16 * T], zz_t[:, 0:16 * T], ACT.Silu).then_inc(s_gate, 1)
                act.wait_ge(s_ct, l + 1)
                nc.scalar.copy(cqh[:, :, :], sq[:, 0:5 * T].rearrange("p (k n) -> p k n", n=T))\
                    .then_inc(s_ch, 1)
                r = RUN[f"up{l}"]
                presplit(f"up{l}")
                split(r, 0, 2)

                def drain_up(i):
                    e = r["e0"] + i
                    par = e % 2
                    if i < 4:
                        act.wait_ge(s_up, 4 * l + i + 1)
                        for half in range(2):
                            n = 512 if (i, half) != (3, 1) else 256
                            at = 1024 * i + 512 * half
                            last = nc.scalar.copy(an_t[:, at:at + n], bank[2 * par + half][:, 0:n])
                    else:
                        act.wait_ge(s_slab, SLABS * r["m0"] + i - 1)
                        n, at = (512, 0) if i == 4 else (256, 512)
                        for t in range(2):
                            last = nc.scalar.copy(va[:, t, at:at + n], bank[2 * par + t][:, 0:n])
                    last.then_inc(s_drain, 2)
                drain_up(0)
                drain_up(1)
                split(r, 0, 3)
                for i in range(2, 6):
                    drain_up(i)
                for h in range(8):
                    act.wait_ge(s_im, 8 * l + h + 1)
                    if h >= 2:
                        act.wait_ge(s_ia, 16 * l + 2 * (h - 1))
                    nc.scalar.activation(pts[:, h % 2, :], bank[5 + h % 2][:, :], ACT.Relu)\
                        .then_inc(s_ir, 1)

                def exps(i):
                    for t in range(2):
                        x = scs[:, i % 3, T * t:T * (t + 1)]
                        c = 2 * (i % 4) + t
                        last = nc.scalar.activation(x, x, ACT.Exp, bias=sm[:, SM_NM + c:SM_NM + c + 1],
                                                    accum_out=sm[:, SM_SUM + c:SM_SUM + c + 1])
                    return last
                softmax_units(N1 * l, N1, exps, lambda i: HAS_T1[i])
                act.wait_ge(s_of, NT1 * (l + 1))
                nc.scalar.activation(sq[:, 0:5 * T], zz_t[:, T * Z_CQ:T * (Z_CQ + 5)], ACT.Square)\
                    .then_inc(s_osq, 1)
                act.wait_ge(s_oss, l + 1)
                for c in range(3):
                    n = 512 if c < 2 else 256
                    last = nc.scalar.activation(sc[:, 512 * c:512 * c + n], bank[5 + c][:, 0:n], ACT.Sqrt,
                                                bias=EPSB, scale=1.0 / P)
                last.then_inc(s_ort, 1)
                r = RUN[f"ple{l}"]
                presplit(f"ple{l}")
                act.wait_ge(s_p, 16 * (l + 1))
                nc.scalar.copy(uhi[:, 0:2, :], praw[:, :, :]).then_inc(s_uh, 4)

                def drain_e(s):
                    act.wait_ge(s_slab, SLABS * r["m0"] + s + 1)
                    par = (r["e0"] + s) % 2
                    for half in range(2):
                        at = T * 16 + 1024 * s + 512 * half
                        last = nc.scalar.copy(zz_t[:, at:at + 512], bank[2 * par + half][:, :])
                    last.then_inc(s_drain, 2)
                for s in range(SLABS):
                    if s + 2 < SLABS:
                        split(r, 0, s + 2)
                    elif s == 2:
                        presplit(f"o{l}")
                    drain_e(s)
                act.wait_ge(s_mix, l + 1)
                fill_u(f"m{l}", zz_t, f"o{l}")
                run(RUN[f"o{l}"], nothing, then=(f"pg{l}",))
                act.wait_ge(*residual(f"o{l}"))
                fill_u(f"g{l}", h_t, f"pg{l}")
                run(RUN[f"pg{l}"], gater(GATED[f"pg{l}"], ACT.Sigmoid, 0))

            def fourier(tag, inv):
                r = RUN[f"f{tag}i"]
                norm("nf" + tag)
                run(r, copier(lambda g, half: zf_t[:, 1024 * g + 512 * half:1024 * g + 512 * half + 512]),
                    0, 4, pre=False, then=(f"f{tag}i", 4))
                for g in range(8):
                    for t in range(2):
                        i = 16 * inv + 2 * g + t
                        act.wait_ge(s_f1, i + 1)
                        if 8 * inv + g >= 2:
                            act.wait_ge(s_f2, 8 * inv + g - 1)
                        nc.scalar.copy(ab[:, g % 2, t, 0:T], bank[5 + t][:, 0:T])
                        nc.scalar.activation(ab[:, g % 2, t, T:2 * T], bank[5 + t][:, T:2 * T], ACT.Copy,
                                             scale=-1.0).then_inc(s_fa, 1)
                run(r, gater(GATED["f" + tag], ACT.Silu, 4), 4, 4, then=(f"f{tag}o",))
                act.wait_ge(s_gu, GATED["f" + tag] + 4)
                fill_u("yf" + tag, zf_t, f"f{tag}o")
                run(RUN[f"f{tag}o"], nothing)

            for l in range(2):
                first_block(l)
            norm("fin")
            fourier("c", 0)
            fourier("x", 1)
            norm("nkc")

            def flat(t, n):
                return lambda g, half: t[:, 2 * half:2 * half + 2, :].rearrange("p k n -> p (k n)")

            def drain_vx(dest):
                def drain(r, g, par):
                    summed(r, g)
                    for t in range(2):
                        last = nc.scalar.copy(dest[:, t, :], bank[2 * par + t][:, 0:T])
                    last.then_inc(s_drain, 2)
                return drain
            run(RUN["kc"], copier(flat(kc, 4)), pre=False, then=("vc",))
            run(RUN["vc"], drain_vx(vc))
            norm("nx1")
            run(RUN["kx"], copier(flat(kx, 4)), pre=False, then=("vx",))
            run(RUN["vx"], drain_vx(vx), then=("qz",))
            run(RUN["qz"], copier(lambda g, half: zq_t[:, bass.ds(g * 1024 + 512 * half, 512)]
                                  if not isinstance(g, int) else
                                  zq_t[:, 1024 * g + 512 * half:1024 * g + 512 * half + 512]))
            act.wait_ge(s_drain, 2 * (RUN["qz"]["e0"] + 8))
            nc.scalar.activation(zq_t[:, 16 * T:32 * T], zq_t[:, 16 * T:32 * T], ACT.Silu)\
                .then_inc(s_gate, 1)

            def exps(i):
                _, h, b = UNITS2[i]
                x = scs[:, i % 3, :]
                c = 2 * (i % 4)
                nc.scalar.activation(x, x, ACT.Exp, bias=sm[:, SM_NM + c:SM_NM + c + 1],
                                     accum_out=sm[:, SM_SUM + c:SM_SUM + c + 1])
                return nc.scalar.activation(sm[:, SM_ES + i % 4:SM_ES + i % 4 + 1], sinkr[:, h:h + 1],
                                            ACT.Exp, bias=sm[:, SM_NM + c:SM_NM + c + 1])
            softmax_units(2 * N1, N2, exps, lambda i: True)
            presplit("ao")
            act.wait_ge(s_of, 2 * NT1 + 16)
            fill_u("ya", zq_t[:, 16 * T:32 * T], "ao")
            run(RUN["ao"], nothing)
            norm("nci")
            r = RUN["ci"]

            def drain_ci(r, g, par):
                summed(r, g)
                if g < 8:
                    if g >= 2:
                        act.wait_ge(s_drain, 2 * (r["e0"] + g - 1))
                    nc.scalar.activation(sq[:, 1024 * (g % 2):1024 * (g % 2) + 512],
                                         bank[2 * par + 1][:, :], ACT.Sigmoid).then_inc(s_cg, 1)
                else:
                    for half in range(2):
                        at = 1024 * (g - 8) + 512 * half
                        last = nc.scalar.activation(zs_t[:, at:at + 512], bank[2 * par + half][:, :],
                                                    ACT.Silu)
                    last.then_inc(s_drain, 2)
            for g in range(12):
                split(r, g, 0)
                split(r, g, 1)
                if g:
                    drain_ci(r, g - 1, (r["e0"] + g - 1) % 2)
                split(r, g, 2)
                split(r, g, 3)
            drain_ci(r, 11, (r["e0"] + 11) % 2)
            for c in range(4):
                act.wait_ge(s_lnr, c + 1)
                if c >= 2:
                    act.wait_ge(s_lns, c)
                nc.scalar.activation(sq[:, 1024 * (c % 2):1024 * (c % 2 + 1)], yc_t[:, 1024 * c:1024 * c + 1024],
                                     ACT.Square).then_inc(s_lnq, 1)
            act.wait_ge(s_lns, 5)
            nc.scalar.activation(sc[:, 0:T], bank[6][:, 0:T], ACT.Sqrt, bias=EPSB, scale=1.0 / D)\
                .then_inc(s_rt2, 1)
            for kt in range(KT):
                if kt % 4 == 0:
                    act.wait_ge(s_lny, kt // 4 + 1)
                nc.scalar.activation(yc[:, kt, :], yc[:, kt, :], ACT.Silu, bias=col("conv_ln_b_2", kt),
                                     scale=col("conv_ln_g_2", kt)).then_inc(s_lnz, 1)
            presplit("co")
            act.wait_ge(s_yc, 1)
            fill_u("yco", yc_t, "co")
            run(RUN["co"], nothing)
            fourier("3", 2)
            norm("end")

        @block.vector
        def _(dve):
            v = nc.vector
            steps = [0]

            def link(ins):
                steps[0] += 1
                ins.then_inc(s_dv, 1)
                dve.wait_ge(s_dv, steps[0])

            def split(r, g, s):
                n = r["width"]
                dve.wait_ge(s_hi, g * SLABS + (SLABS * r["m0"] + s + 1))
                v.tensor_tensor(wlo[:, s % 2, 0:n], raw[:, s, 0:n], whi[:, s % 2, 0:n].bitcast(F32),
                                ALU.subtract).then_inc(s_lo, 1)

            def presplit(name, g=0):
                split(RUN[name], g, 0)
                split(RUN[name], g, 1)

            def summed(r, g):
                dve.wait_ge(s_slab, (g + (r["m0"] + 1)) * SLABS)

            def run(r, drain, g0=0, n=None, pre=True, then=None):
                n = r["n"] if n is None else n
                if not pre:
                    split(r, g0, 0)
                    split(r, g0, 1)
                split(r, g0, 2)
                split(r, g0, 3)

                def body(g, par):
                    split(r, g, 0)
                    split(r, g, 1)
                    drain(r, g - 1, par)
                    split(r, g, 2)
                    split(r, g, 3)
                pairs = (n - 1) // 2
                if pairs > 1:
                    with dve.Fori(0, pairs) as j:
                        for half in range(2):
                            body(j * 2 + (g0 + 1 + half), (r["e0"] + g0 + half) % 2)
                else:
                    for g in range(1, 1 + 2 * pairs):
                        body(g0 + g, (r["e0"] + g0 + g - 1) % 2)
                if (n - 1) % 2:
                    body(g0 + n - 1, (r["e0"] + g0 + n - 2) % 2)
                if then is not None:
                    presplit(*then)
                drain(r, g0 + n - 1, (r["e0"] + g0 + n - 1) % 2)

            def nothing(r, g, par):
                pass

            def adder(dest_t, gate):
                def drain(r, g, par):
                    summed(r, g)
                    if gate is None:
                        for half in range(2):
                            at = 1024 * g + 512 * half
                            last = v.tensor_tensor(dest_t[:, at:at + 512], bank[2 * par + half][:, :],
                                                   dest_t[:, at:at + 512], ALU.add)
                    else:
                        for b in range(4):
                            at = 1024 * g + T * b
                            last = v.scalar_tensor_tensor(
                                out=dest_t[:, at:at + T],
                                in0=bank[2 * par + b // 2][:, T * (b % 2):T * (b % 2) + T],
                                scalar=gate(4 * g + b), in1=dest_t[:, at:at + T],
                                op0=ALU.mult, op1=ALU.add)
                    last.then_inc(s_drain, 2)
                return drain

            def norm(name):
                n = NORMS[name]
                src = NORM_ARGS[name][0]
                source_ready(dve, name)
                dve.wait_ge(s_rt, n + 1)
                rr = sc[:, 1024:1024 + T]
                link(v.reciprocal(rr, rr))
                if name in ("fin", "end"):
                    dest, signal = (hh, s_fin) if name == "fin" else (zf, s_yd)
                    for kt in range(KT):
                        last = v.scalar_tensor_tensor(out=dest[:, kt, :], in0=src[:, kt, :],
                                                      scalar=norm_scale(name, kt), in1=rr,
                                                      op0=ALU.mult, op1=ALU.mult)
                        if kt % 4 == 3 and (name == "end" or kt == KT - 1):
                            last.then_inc(signal, 1)
                    return

                def lo(kt):
                    dve.wait_ge(s_nh, 16 * U_NORMS[name] + kt + 1)
                    sh = norm_shift(name, kt)
                    if sh is None:
                        last = v.tensor_tensor(ulo[:, kt, :], tt4[:, kt % 4, :],
                                               uhi[:, kt, :].bitcast(F32), ALU.subtract)
                    else:
                        last = v.scalar_tensor_tensor(out=ulo[:, kt, :], in0=tt4[:, kt % 4, :],
                                                      scalar=sh, in1=uhi[:, kt, :].bitcast(F32),
                                                      op0=ALU.add, op1=ALU.subtract)
                    last.then_inc(s_nl, 1)
                for kt in range(KT):
                    if kt >= 4:
                        dve.wait_ge(s_nl, 16 * U_NORMS[name] + kt - 3)
                    v.scalar_tensor_tensor(out=tt4[:, kt % 4, :], in0=src[:, kt, :],
                                           scalar=norm_scale(name, kt), in1=rr,
                                           op0=ALU.mult, op1=ALU.mult).then_inc(s_nt, 1)
                    if kt >= 2:
                        lo(kt - 2)
                lo(KT - 2)
                lo(KT - 1)

            def fill_u(name, src, chunks=4, width=1024, inc=1):
                for c in range(chunks):
                    dve.wait_ge(s_uh, 4 * SPLITS[name] + c + 1)
                    v.tensor_tensor(ulo_t[:, width * c:width * (c + 1)], src[:, width * c:width * (c + 1)],
                                    uhi_t[:, width * c:width * (c + 1)].bitcast(F32),
                                    ALU.subtract).then_inc(s_ul, inc)

            def ropes(jobs, base_job, table):
                def sums(i):
                    x, _, nb = jobs[i]
                    r = pt[:, 512 * (i % 2):512 * (i % 2) + T * nb]
                    dve.wait_ge(s_dv, need[i])
                    v.tensor_tensor(x, x, r, ALU.add).then_inc(s_ro, 1)
                need = {}
                for i, (x, kind, nb) in enumerate(jobs):
                    cos, sin = table(kind, nb)
                    r = pt[:, 512 * (i % 2):512 * (i % 2) + T * nb]
                    dve.wait_ge(s_rm, base_job + i + 1)
                    if i >= 2:
                        dve.wait_ge(s_ro, base_job + i - 1)
                    as3 = lambda a, nb=nb: a.rearrange("p (k n) -> p k n", k=nb)
                    v.tensor_tensor(as3(r), as3(bank[5 + i % 2][:, 0:T * nb]), sin, ALU.mult)
                    v.tensor_tensor(as3(x), as3(x), cos, ALU.mult).then_inc(s_dv, 1)
                    steps[0] += 1
                    need[i] = steps[0]
                    if i:
                        sums(i - 1)
                sums(len(jobs) - 1)

            def softmax_units(first, n, maxes, scales, outs):
                for t in range(n + 3):
                    if t < n:
                        u = first + t
                        dve.wait_ge(s_s, u + 1)
                        if t >= 3:
                            dve.wait_ge(s_t, TN[u - 3])
                            dve.wait_ge(s_pr, u - 1)
                        maxes(t, u)
                    if 1 <= t <= n:
                        u = first + t - 1
                        dve.wait_ge(s_e, u + 1)
                        scales(t - 1).then_inc(s_pr, 1)
                    if t >= 3:
                        outs(t - 3, TN[first + t - 3])

            dve.wait_ge(s_in, 16 * INPUT_DMAS)
            lv = lamr[:, :].rearrange("p (l q n) -> p l q n", l=2, q=4)
            lp = sq[:, 0:256].rearrange("p (l q n) -> p l q n", l=2, q=2)
            for l in range(2):
                last = v.tensor_tensor(lp[:, l], lv[:, l, 0:4:2], lv[:, l, 1:4:2], ALU.mult)
            link(last)
            v.tensor_reduce(sm[:, SM_TMP:SM_TMP + 4], sq[:, 0:256].rearrange("p (a n) -> p a n", n=64),
                            AX.X, ALU.add).then_inc(s_lam, 1)
            link(v.tensor_copy(ang[:, 0:T], posi[:, :]))
            for k in (2, 1, 0):
                last = v.tensor_scalar(ang[:, T * k:T * (k + 1)], ang[:, 0:T],
                                       kk[:, K_INVF + k:K_INVF + k + 1], None, ALU.mult)
            link(last)
            TWO_PI = 2 * math.pi
            C1 = 6.28125
            C2 = float(np.float32(np.round((TWO_PI - C1) * 2 ** 20) / 2 ** 20))
            C3 = TWO_PI - C1 - C2
            ROUND = 12582912.0
            PI32 = 3.1415925
            for i, (turn, back) in enumerate(((0.25, math.pi / 2), (0.0, 0.0))):
                link(v.tensor_scalar(trn[:, :], ang[:, :], 1 / TWO_PI, turn, ALU.mult, ALU.add))
                link(v.tensor_scalar(trn[:, :], trn[:, :], ROUND, None, ALU.add))
                link(v.tensor_scalar(trn[:, :], trn[:, :], -ROUND, None, ALU.add))
                if i:
                    dve.wait_ge(s_tab, 1)
                link(v.scalar_tensor_tensor(out=red[:, :], in0=trn[:, :], scalar=-C1, in1=ang[:, :],
                                            op0=ALU.mult, op1=ALU.add))
                link(v.scalar_tensor_tensor(out=red[:, :], in0=trn[:, :], scalar=-C2, in1=red[:, :],
                                            op0=ALU.mult, op1=ALU.add))
                link(v.scalar_tensor_tensor(out=red[:, :], in0=trn[:, :], scalar=-C3, in1=red[:, :],
                                            op0=ALU.mult, op1=ALU.add))
                link(v.tensor_scalar(red[:, :], red[:, :], back, PI32, ALU.add, ALU.min))
                v.tensor_scalar(red[:, :], red[:, :], -PI32, None, ALU.max).then_inc(s_sin, 1)
            dve.wait_ge(s_lam, 2)
            for l in range(2):
                a = SM_TMP + 4 + 2 * l
                link(v.tensor_tensor(sm[:, SM_LAM + l:SM_LAM + l + 1], sm[:, a + 1:a + 2], sm[:, a:a + 1],
                                     ALU.subtract))
                v.tensor_scalar(sm[:, SM_LAM + l:SM_LAM + l + 1], sm[:, SM_LAM + l:SM_LAM + l + 1],
                                -LAM_INIT[l], None, ALU.add)
                link(v.tensor_scalar(sm[:, SM_SUBG + l:SM_SUBG + l + 1], col("subln_g", l),
                                     1.0 - LAM_INIT[l], None, ALU.mult))
            dve.wait_ge(s_tab, 2)

            def modulation(l):
                dve.wait_ge(s_ada, SLABS * next(g for m, g in MOD_READS if l < m))
                bias = col("ada_b_2", 48 * l, 48).unsqueeze(2).broadcast_to([P, 48, 2])
                link(v.tensor_tensor(mods[:, l], bank[4][:, 96 * l:96 * l + 96]
                                     .rearrange("p (b c) -> p b c", c=2), bias, ALU.add))
                for c in range(2):
                    last = v.scalar_tensor_tensor(out=gs[:, 32 * l + 16 * c:32 * l + 16 * c + 16],
                                                  in0=mods[:, l, 16:32, c], scalar=1.0,
                                                  in1=col("norm_g_2", 16 * l, 16),
                                                  op0=ALU.add, op1=ALU.mult)
                last.then_inc(s_mod, 1)
                dve.wait_ge(s_mod, l + 1)

            def first_block(l):
                norm(f"n{l}")
                run(RUN[f"in{l}"], nothing, pre=False, then=(f"v{l}",))
                run(RUN[f"v{l}"], nothing)
                dve.wait_ge(s_crt, l + 1)
                link(v.reciprocal(sc[:, 0:512], sc[:, 0:512]))
                for k in range(5):
                    g = col("q_norm_g", 3 * l + k) if k < 3 else col("kv_norm_g", 2 * l + k - 3)
                    last = v.scalar_tensor_tensor(out=sq[:, T * k:T * (k + 1)], in0=zz[:, Z_CQ + k, :],
                                                  scalar=g, in1=sc[:, T * (k > 2):T * (k > 2) + T],
                                                  op0=ALU.mult, op1=ALU.mult)
                last.then_inc(s_ct, 1)
                dve.wait_ge(s_ch, l + 1)
                v.tensor_tensor(cql[:, :, :], sq[:, 0:5 * T].rearrange("p (k n) -> p k n", n=T),
                                cqh[:, :, :].bitcast(F32), ALU.subtract).then_inc(s_cl, 1)

                def table(kind, nb):
                    return [tabs[:, 2 * kind + i:2 * kind + i + 1, :].broadcast_to([P, nb, T])
                            for i in range(2)]
                jobs = rope_jobs()
                ropes(jobs[:14], NJ * l, table)
                r = RUN[f"up{l}"]
                for s in range(SLABS):
                    split(r, 0, s)
                dve.wait_ge(s_drain, 2 * (r["e0"] + 6))
                ropes(jobs[14:], NJ * l + 14, table)
                acc = [sq[:, 1024 + T * t:1024 + T * (t + 1)] for t in range(2)]
                for h in range(8):
                    dve.wait_ge(s_ir, 8 * l + h + 1)
                    if h:
                        dve.wait_ge(s_ia, 16 * l + 2 * h)
                    for t in range(2):
                        x = pts[:, h % 2, T * t:T * (t + 1)]
                        wcol = vv[:, t, V_W + h:V_W + h + 1]
                        if h == 0:
                            ins = v.tensor_scalar(acc[t], x, wcol, None, ALU.mult)
                        else:
                            ins = v.scalar_tensor_tensor(out=acc[t], in0=x, scalar=wcol, in1=acc[t],
                                                         op0=ALU.mult, op1=ALU.add)
                        ins.then_inc(s_ia, 1)
                dve.wait_ge(s_ia, 16 * l + 16)
                work = sq[:, 512:1024]
                link(v.tensor_tensor(work, sq[:, 1024:1536], mask1, ALU.add))
                for i in range(TOPK // 8):
                    m8 = [sm[:, SM_M8 + 8 * t:SM_M8 + 8 * t + 8] for t in range(2)]
                    for t in range(2):
                        last = v.max(m8[t], work[:, T * t:T * (t + 1)])
                    link(last)
                    for t in range(2):
                        x = work[:, T * t:T * (t + 1)]
                        last = v.match_replace(x, m8[t], x, TAKEN)
                    link(last)
                bm = sq[:, 0:512]
                link(v.tensor_scalar(bm, work, TAKEN / 2, NEG, ALU.is_gt, ALU.mult))
                link(v.tensor_tensor(bm, bm, mask1, ALU.add))

                def maxes(i, u):
                    m = UNITS1[i][0]
                    x = scs[:, i % 3, :]
                    scale = {"a": 192 ** -0.5, "b": P ** -0.5, "c": 64 ** -0.5}[m]
                    v.scalar_tensor_tensor(out=x, in0=bank[i % 2][:, :], scalar=scale,
                                           in1=bm if m == "b" else mask1, op0=ALU.mult,
                                           op1=ALU.add).then_inc(s_sd, 1)
                    dve.wait_ge(s_sd, u + 1)
                    c = SM_NM + 2 * (i % 4)
                    v.tensor_reduce(sm[:, c:c + 2], x.rearrange("p (t n) -> p t n", t=2), AX.X, ALU.max,
                                    negate=True).then_inc(s_m, 1)

                def scales(i):
                    m, h, part = UNITS1[i]
                    c = 2 * (i % 4)
                    ri = sm[:, SM_RI + c:SM_RI + c + 2]
                    link(v.reciprocal(ri, sm[:, SM_SUM + c:SM_SUM + c + 2]))
                    x = scs[:, i % 3, :].rearrange("p (t n) -> p t n", t=2)
                    if part == 0:
                        return v.tensor_tensor(x, x, ri.unsqueeze(2).broadcast_to([P, 2, T]), ALU.mult)
                    rl = sm[:, SM_RL + c:SM_RL + c + 2]
                    link(v.tensor_scalar(rl, ri, sm[:, SM_LAM + l:SM_LAM + l + 1], None, ALU.mult))
                    for t in range(2):
                        last = v.scalar_tensor_tensor(out=x[:, t], in0=x[:, t], scalar=rl[:, t:t + 1],
                                                      in1=scs[:, (i - 1) % 3, T * t:T * (t + 1)],
                                                      op0=ALU.mult, op1=ALU.add)
                    return last

                def outs(i, tn):
                    m, h, part = UNITS1[i]
                    if not HAS_T1[i]:
                        return
                    dve.wait_ge(s_o, tn)
                    o = bank[5 + (tn - 1) % 2][:, 0:T]
                    if m == "c":
                        v.tensor_copy(zz[:, Z_CQ + h, :], o).then_inc(s_of, 1)
                    else:
                        g = zz[:, h if m == "a" else 6 + h, :]
                        v.tensor_tensor(g, o, g, ALU.mult).then_inc(s_of, 1)
                dve.wait_ge(s_gate, l + 1)
                softmax_units(N1 * l, N1, maxes, scales, outs)
                dve.wait_ge(s_ort, l + 1)
                link(v.reciprocal(sc[:, 0:5 * T], sc[:, 0:5 * T]))
                oc = zz_t[:, T * Z_CQ:T * (Z_CQ + 5)]
                link(v.scalar_tensor_tensor(out=oc, in0=oc, scalar=sm[:, SM_SUBG + l:SM_SUBG + l + 1],
                                            in1=sc[:, 0:5 * T], op0=ALU.mult, op1=ALU.mult))
                gc = zz_t[:, T * 11:T * 16]
                v.tensor_tensor(gc, gc, oc, ALU.mult).then_inc(s_mix, 1)
                presplit(f"ple{l}")
                fill_u(f"p{l}", praw[:, :, :].rearrange("p k n -> p (k n)"), 1, 512, 4)
                r = RUN[f"ple{l}"]
                split(r, 0, 2)
                split(r, 0, 3)
                presplit(f"o{l}")
                fill_u(f"m{l}", zz_t)
                run(RUN[f"o{l}"], adder(h_t, None), then=(f"pg{l}",))
                fill_u(f"g{l}", h_t)

                def drain_pg(r, g, par):
                    i = GATED[f"pg{l}"] + g
                    dve.wait_ge(s_drain, 2 * (r["e0"] + g + 1))
                    x = sq[:, 1024 * (i % 2):1024 * (i % 2) + 1024]
                    link(v.tensor_tensor(x, x, zz_t[:, T * 16 + 1024 * g:T * 16 + 1024 * g + 1024],
                                         ALU.mult))
                    y = h_t[:, 1024 * g:1024 * g + 1024]
                    v.tensor_tensor(y, y, x, ALU.add).then_inc(s_gu, 1)
                run(RUN[f"pg{l}"], drain_pg)

            def fourier(tag, inv, dest_t, l, cond):
                r = RUN[f"f{tag}i"]
                norm("nf" + tag)
                run(r, nothing, 0, 4, pre=False, then=(f"f{tag}i", 4))
                for g in range(8):
                    dve.wait_ge(s_f2, 8 * inv + g + 1)
                    v.tensor_copy(zf_t[:, 512 * g:512 * g + 512], bank[7][:, :]).then_inc(s_fb, 1)
                dve.wait_ge(s_fb, 8 * inv + 8)

                def drain_z(r, g, par):
                    i = GATED["f" + tag] + g - 4
                    dve.wait_ge(s_drain, 2 * (r["e0"] + g + 1))
                    y = zf_t[:, 1024 * (g - 4):1024 * (g - 4) + 1024]
                    v.tensor_tensor(y, y, sq[:, 1024 * (i % 2):1024 * (i % 2) + 1024], ALU.mult)\
                        .then_inc(s_gu, 1)
                run(r, drain_z, 4, 4, then=(f"f{tag}o",))
                fill_u("yf" + tag, zf_t)
                run(RUN[f"f{tag}o"], adder(dest_t, lambda b: mods[:, l, 32 + b, cond:cond + 1]))

            for l in range(2):
                first_block(l)
            modulation(0)
            modulation(1)
            norm("fin")
            fourier("c", 0, cc_t, 0, 1)
            fourier("x", 1, h_t, 0, 0)
            norm("nkc")
            run(RUN["kc"], nothing, pre=False, then=("vc",))
            run(RUN["vc"], nothing)
            norm("nx1")
            run(RUN["kx"], nothing, pre=False, then=("vx",))
            run(RUN["vx"], nothing, then=("qz",))
            run(RUN["qz"], nothing)
            dve.wait_ge(s_drain, 2 * (RUN["qz"]["e0"] + 8))

            def table(kind, nb):
                return [k2[:, K2_AX + T * i:K2_AX + T * (i + 1)].unsqueeze(1).broadcast_to([P, nb, T])
                        for i in range(2)]
            ropes(rope_jobs_x(), 2 * NJ, table)
            nsink = lamr[:, 0:32]
            link(v.tensor_scalar(nsink, sinkr[:, :], -1.0, None, ALU.mult))

            def maxes(i, u):
                _, h, b = UNITS2[i]
                x = scs[:, i % 3, :]
                v.scalar_tensor_tensor(out=x, in0=bank[i % 2][:, :], scalar=0.125, in1=mask2[:, b],
                                       op0=ALU.mult, op1=ALU.add).then_inc(s_sd, 1)
                dve.wait_ge(s_sd, u + 1)
                c = SM_NM + 2 * (i % 4)
                link(v.tensor_reduce(sm[:, c:c + 1], x, AX.X, ALU.max, negate=True))
                v.tensor_tensor(sm[:, c:c + 1], sm[:, c:c + 1], nsink[:, h:h + 1], ALU.min)\
                    .then_inc(s_m, 1)

            def scales(i):
                c = 2 * (i % 4)
                ri = sm[:, SM_RI + c:SM_RI + c + 1]
                link(v.tensor_tensor(ri, sm[:, SM_SUM + c:SM_SUM + c + 1],
                                     sm[:, SM_ES + i % 4:SM_ES + i % 4 + 1], ALU.add))
                link(v.reciprocal(ri, ri))
                x = scs[:, i % 3, :]
                return v.tensor_scalar(x, x, ri, None, ALU.mult)

            def outs(i, tn):
                if i % 4 != 3:
                    return
                dve.wait_ge(s_o, tn)
                hp = i // 4
                g = zq[:, 16 + hp, :]
                v.tensor_tensor(g, bank[5 + hp % 2][:, 0:T], g, ALU.mult).then_inc(s_of, 1)
            dve.wait_ge(s_gate, 3)
            softmax_units(2 * N1, N2, maxes, scales, outs)
            modulation(2)
            presplit("ao")
            fill_u("ya", zq_t[:, 16 * T:32 * T])
            run(RUN["ao"], adder(h_t, lambda b: mods[:, 1, 32 + b, 0:1]))
            v.memset(gp[:, :, 0:15], 0.0)
            link(v.memset(gp[:, :, 15 + T:PADT], 0.0))
            norm("nci")
            r = RUN["ci"]
            TAPS = 31

            def conv_steps():
                for k in range(0, KT, 2):
                    for t in range(TAPS):
                        for b in (k, k + 1):
                            x = gp[:, b, t:t + T]
                            wt = col("conv_dw_w_2", 16 * t + b)
                            yield b, t, x, wt
            conv = conv_steps()

            def conv_some(n):
                for _ in range(n):
                    s = next(conv, None)
                    if s is None:
                        return
                    b, t, x, wt = s
                    if t == 0:
                        if b % 2 == 0:
                            dve.wait_ge(s_drain, 2 * (r["e0"] + b // 2 + 1))
                        ins = v.tensor_scalar(yc[:, b, :], x, wt, col("conv_dw_b_2", b), ALU.mult, ALU.add)
                    else:
                        dve.wait_ge(s_dv, steps[0] - (0 if t == TAPS - 1 and b % 2 else 1))
                        ins = v.scalar_tensor_tensor(out=yc[:, b, :], in0=x, scalar=wt, in1=yc[:, b, :],
                                                     op0=ALU.mult, op1=ALU.add)
                    if t < TAPS - 1:
                        steps[0] += 1
                        ins.then_inc(s_dv, 1)
                    else:
                        ins.then_inc(s_conv, 1)

            def drain_ci(g):
                if g >= 8:
                    return
                par = (r["e0"] + g) % 2
                dve.wait_ge(s_cg, g + 1)
                v.tensor_tensor(gp[:, 2 * g:2 * g + 2, 15:15 + T],
                                bank[2 * par][:, :].rearrange("p (k n) -> p k n", k=2),
                                sq[:, 1024 * (g % 2):1024 * (g % 2) + 512]
                                .rearrange("p (k n) -> p k n", k=2), ALU.mult).then_inc(s_drain, 2)
            for g in range(12):
                some = 12 if g >= 2 else 0
                split(r, g, 0)
                conv_some(some)
                split(r, g, 1)
                if g:
                    drain_ci(g - 1)
                conv_some(some)
                split(r, g, 2)
                conv_some(some)
                split(r, g, 3)
                conv_some(some)
            conv_some(1000)
            dve.wait_ge(s_lns, 1)
            mu = sc[:, 512:768]
            link(v.tensor_scalar(mu, bank[5][:, 0:T], 1.0 / D, None, ALU.mult))
            mu4 = mu.unsqueeze(1).broadcast_to([P, 4, T])
            for c in range(4):
                y = yc[:, 4 * c:4 * c + 4, :]
                v.tensor_tensor(y, y, mu4, ALU.subtract).then_inc(s_lnr, 1)
            dve.wait_ge(s_rt2, 1)
            link(v.reciprocal(sc[:, 0:T], sc[:, 0:T]))
            r4 = sc[:, 0:T].unsqueeze(1).broadcast_to([P, 4, T])
            dve.wait_ge(s_lnr, 4)
            for c in range(4):
                y = yc[:, 4 * c:4 * c + 4, :]
                v.tensor_tensor(y, y, r4, ALU.mult).then_inc(s_lny, 1)
            for c in range(4):
                dve.wait_ge(s_lnz, 4 * c + 4)
                if c == 0:
                    dve.wait_ge(s_drain, 2 * (r["e0"] + 12))
                y = yc_t[:, 1024 * c:1024 * c + 1024]
                last = v.tensor_tensor(y, y, zs_t[:, 1024 * c:1024 * c + 1024], ALU.mult)
            last.then_inc(s_yc, 1)
            presplit("co")
            fill_u("yco", yc_t)
            run(RUN["co"], adder(h_t, lambda b: mods[:, 2, 32 + b, 0:1]))
            modulation(3)
            fourier("3", 2, h_t, 3, 0)
            norm("end")


def slabs_of(w, col_blocks):
    w = np.asarray(w)
    n = len(col_blocks)
    assert n % 4 == 0
    out = np.zeros((n // 4, SLABS, P, 4, 4, P), w.dtype)
    v = w.reshape(SLABS, 4, P, w.shape[1])
    for b, c in enumerate(col_blocks):
        if c is None:
            continue
        pieces = c if isinstance(c, list) else [(c, P)]
        at = 0
        for c0, m in pieces:
            out[b // 4, :, :, :, b % 4, at:at + m] = v[:, :, :, c0:c0 + m].transpose(0, 2, 1, 3)
            at += m
    return out.reshape(n // 4, SLABS, P, 2048)


def tiles_of(tiles, dtype):
    out = np.zeros((SLABS, P, 16, P), dtype)
    for i, t in enumerate(tiles):
        if t is not None:
            out[i // 16, :, i % 16, :] = t
    return out.reshape(SLABS, P, 2048)


def run_of(c0, n):
    return [c0 + P * i for i in range(n)]


def host_weights(a):
    out = {}
    win, wv, wup, wple = [], [], [], []
    for l in range(2):
        w = a["w_in"][l]
        blocks = (run_of(704, 6) + run_of(3976, 5) + run_of(6536, 5)
                  + run_of(1472, 5) + run_of(2112, 5) + run_of(3392, 4) + [[(3904, 64), (3904, 64)]]
                  + run_of(4616, 5) + run_of(5256, 5) + run_of(0, 5) + [[(640, 64), (640, 64)]] + [None])
        win.append(slabs_of(w, blocks))
        vb = run_of(2752, 5) + [[(3968, 8), (5896, 120)]] + run_of(5896 + 120, 4) + [[(6528, 8)]] + [None]
        wv.append(slabs_of(w, vb))
        q = a["w_uq"][l].reshape(3, P, 1152)
        kv = a["w_ukv"][l].reshape(2, P, 1536)
        t = []
        qcols = [[(192 * h, P)] for h in range(6)]
        qcols += [[(192 * h + P, 64), (192 * (h + 1) + P, 64)] for h in (0, 2, 4)]
        for b in range(9):
            for k in range(3):
                t.append(np.concatenate([q[k][:, c:c + n] for c, n in qcols[b]], axis=1))
            if b == 4:
                t.append(None)
        for h in range(6):
            for k in range(2):
                t.append(kv[k][:, T * h:T * h + P])
        for h0, h1 in ((0, 4), (4, 6)):
            for k in range(2):
                for h in range(h0, h1):
                    t.append(kv[k][:, T * h + P:T * h + 2 * P])
        wup.append(tiles_of(t, q.dtype)[None])
        e = a["w_ple"][l].reshape(2, P, 4, 4, P)
        ple = np.zeros((SLABS, P, 16, P), e.dtype)
        ple[:, :, 0:8, :] = e.transpose(2, 1, 0, 3, 4).reshape(SLABS, P, 8, P)
        wple.append(ple.reshape(1, SLABS, P, 2048))
    out["win"], out["wv"] = np.concatenate(win), np.concatenate(wv)
    out["wup"], out["wple"] = np.concatenate(wup), np.concatenate(wple)
    full = run_of(0, 16)
    out["wo"] = np.concatenate([slabs_of(a["w_o"][l], full) for l in range(2)])
    out["wpg"] = np.concatenate([slabs_of(a["w_pg"][l], full) for l in range(2)])
    out["ada"] = np.concatenate([slabs_of(a["ada_w_2"][l], run_of(0, 48)) for l in range(4)])
    out["wfi"] = np.concatenate([slabs_of(a["four_w_in_2"][l], run_of(0, 32)) for l in range(2)])
    out["wfo"] = np.concatenate([slabs_of(a["four_w_out_2"][l], full) for l in range(2)])
    w = a["attn_w_in_2"][0]
    out["wk"] = slabs_of(w, [[(2048 + 64 * j, 64), (2048 + 64 * j, 64)] for j in range(4)])
    out["wvx"] = slabs_of(w, run_of(2304, 2) + [None, None])
    out["wqz"] = slabs_of(w, run_of(0, 16) + run_of(2560, 16))
    out["wao"] = slabs_of(a["attn_w_out_2"][0], full)
    ci = [c for g in range(8) for c in (256 * g, 256 * g + P, D + 256 * g, D + 256 * g + P)]
    out["wci"] = slabs_of(a["conv_w_in_2"][0], ci + run_of(2 * D, 16))
    out["wco"] = slabs_of(a["conv_w_out_2"][0], full)
    return out


def rotation(half, period):
    m = np.zeros((P, P), np.float32)
    for o in range(0, P, period):
        for i in range(half):
            m[o + i + half, o + i] = -1.0
            m[o + i, o + i + half] = 1.0
    return m


def host_constants():
    kk = np.zeros((P, K_N), np.float32)
    kk[:, K_ID:K_ID + P] = np.eye(P)
    for i, (half, period) in enumerate(((32, 64), (16, P), (8, 64), (16, 32))):
        kk[:, K_ROT + P * i:K_ROT + P * (i + 1)] = rotation(half, period)
    q, key = np.arange(P)[:, None], np.arange(T)[None, :]
    for t in range(2):
        seen = key // 64 <= (q + P * t) // 64
        kk[:, K_MASK + T * t:K_MASK + T * (t + 1)] = np.where(seen, 0.0, NEG)
    for i, (half, period) in enumerate(((32, 64), (16, P), (8, 64))):
        f = np.float32(1.0) / np.float32(500000.0) ** (np.arange(half, dtype=np.float32)
                                                      * np.float32(2.0 / (2 * half)))
        for o in range(0, P, period):
            kk[o:o + half, K_INVF + i] = f
            kk[o + half:o + 2 * half, K_INVF + i] = f
    k2 = np.zeros((P, K2_N), np.float32)
    n = np.arange(T)
    angle = 2 * np.pi * (n[:, None] * n[None, :] % T) / T
    for k in range(2):
        rows = slice(P * k, P * (k + 1))
        k2[:, 512 * k:512 * k + T] = np.cos(angle[rows]) / 16
        k2[:, 512 * k + T:512 * k + 512] = np.sin(angle[rows]) / 16
    inv = np.float32(10000.0) ** (-np.arange(16, dtype=np.float32) / np.float32(16))
    row, column = (n // 64).astype(np.float32), (n % 64).astype(np.float32)
    ar, ac = row[:, None] * inv[None, :], column[:, None] * inv[None, :]
    full = np.concatenate([ar, ar, ac, ac], axis=1)
    full = np.concatenate([full, full], axis=1).T
    k2[:, K2_AX:K2_AX + T] = np.cos(full.astype(np.float64))
    k2[:, K2_AX + T:K2_AX + 2 * T] = np.sin(full.astype(np.float64))
    for b in range(2):
        near = np.abs(q + P * b - key) <= 128
        k2[:, K2_MASK + 512 * b:K2_MASK + 512 * b + T] = np.where(near, 0.0, NEG)
    return kk, k2


def transposed(x):
    x = np.asarray(x)
    return np.ascontiguousarray(x.reshape(T, -1, P).transpose(2, 1, 0))


def kernel(**inputs):
    import concourse.bacc as bacc
    from concourse.bass_utils import run_bass_kernel_spmd

    a = {k: np.asarray(v) for k, v in inputs.items()}
    arrays = {"w_" + k: v for k, v in host_weights(a).items()}
    cols = np.concatenate([np.asarray(a[name]).reshape(-1, P) for name in COL], axis=0)
    assert cols.shape[0] == NCOL
    arrays["cols"] = np.ascontiguousarray(cols.T)
    arrays["x"] = transposed(a["x"][0])
    arrays["ctx"] = transposed(a["ctx_2"][0])
    arrays["p"] = np.stack([transposed(a["p"][l, 0]) for l in range(2)])
    lam = np.stack([np.stack([a[n][l] for n in ("lam_q1", "lam_k1", "lam_q2", "lam_k2")])
                    for l in range(2)])
    arrays["lam"] = np.ascontiguousarray(np.broadcast_to(lam.reshape(1, -1), (P, 512)))
    arrays["sink"] = np.ascontiguousarray(np.broadcast_to(a["attn_sink_2"].reshape(1, 32), (P, 32)))
    arrays["pos"] = np.ascontiguousarray(np.broadcast_to(a["positions"].reshape(1, T), (P, T)))
    arrays["eps"] = np.full((P, 1), EPS, np.float32)
    arrays["consts"], arrays["consts2"] = host_constants()

    nc = bacc.Bacc("TRN2", target_bir_lowering=False, num_devices=1)
    aps = {n: nc.dram_tensor(n + "_dram", v.shape, mybir.dt.from_np(v.dtype), kind="ExternalInput").ap()
           for n, v in arrays.items()}
    out = nc.dram_tensor("out_dram", (P, KT, T), F32, kind="ExternalOutput").ap()
    build(nc, {n[2:]: ap for n, ap in aps.items() if n.startswith("w_")}, aps, out)
    r = run_bass_kernel_spmd(nc, [{n + "_dram": v for n, v in arrays.items()}], core_ids=[0])
    got = r.results[0]["out_dram"]
    return np.ascontiguousarray(np.asarray(got).transpose(2, 1, 0)).reshape(1, T, D)
```

```python
import math
from contextlib import ExitStack

import numpy as np
import concourse.bass as bass
from concourse import mybir

F32 = mybir.dt.float32
F32R = mybir.dt.float32r
I32 = mybir.dt.int32
ALU = mybir.AluOpType
ACT = mybir.ActivationFunctionType
AX = mybir.AxisListType

P = 128
D = 2048
KT = D // P
T = 256
EPS = 1e-6
NEG = -1e30
TAKEN = -3e38
SLABS = 4
TOPK = min(256, T // 4)
ADA_GROUPS = 48
ADA_BOTH = 24
LAM_INIT = [0.8 - 0.6 * math.exp(-0.3 * i) for i in range(2)]

Z_GATE = 0
Z_QB, Z_KB, Z_QI, Z_KI, Z_QC, Z_KC, Z_CQ, Z_CKV, Z_KR = 16, 21, 26, 30, 31, 36, 41, 44, 46
V_B, V_W, V_C = 0, 640, 648
V_COLS = 1288
AN_QR, AN_KN = 6, 9

K_ID, K_ROT, K_MASK, K_INVF, K_N = 0, 128, 640, 1152, 1155
K2_DFT, K2_AX, K2_MASK, K2_N = 0, 1024, 1536, 2560


def column_fields():
    sizes = [("norm_g", 32), ("q_norm_g", 6), ("kv_norm_g", 4), ("subln_g", 2), ("final_g", 16),
             ("norm_g_2", 64), ("ada_b_2", 192), ("conv_dw_b_2", 16), ("conv_ln_g_2", 16),
             ("conv_ln_b_2", 16), ("final_g_2", 16), ("c_2", 16), ("c_ctx_2", 16),
             ("conv_dw_w_2", 31 * 16)]
    at, out = 0, {}
    for name, n in sizes:
        out[name] = at
        at += n
    return out, at


COL, NCOL = column_fields()


def stream_plan():
    runs = []

    def run(name, kind, weights, first, groups, steps=None, width=2048, ada=1):
        runs.append(dict(name=name, kind=kind, w=weights, first=first, n=groups,
                         steps=groups if steps is None else steps, width=width, ada=ada))

    for l in range(2):
        run(f"in{l}", "T", "win", 12 * l, 12)
        run(f"v{l}", "N", "wv", 3 * l, 3)
        run(f"up{l}", "S", "wup", l, 1, 6, ada=0)
        run(f"ple{l}", "E", "wple", l, 1, 4, 1024, ada=0)
        run(f"o{l}", "T", "wo", 4 * l, 4)
        run(f"pg{l}", "T", "wpg", 4 * l, 4)
    for which, j in (("fc", 0), ("fx", 0), ("f3", 1)):
        if which == "f3":
            run("kc", "T", "wk", 0, 1, ada=2)
            run("vc", "N", "wvx", 0, 1, ada=0)
            run("kx", "T", "wk", 0, 1, ada=2)
            run("vx", "N", "wvx", 0, 1, ada=0)
            run("qz", "T", "wqz", 0, 8)
            run("ao", "T", "wao", 0, 4, ada=2)
            run("ci", "T", "wci", 0, 12, ada=0)
            run("co", "T", "wco", 0, 4, ada=2)
        left = 1 if which != "f3" else 0
        run(which + "i", "T", "wfi", 8 * j, 8, ada=left)
        run(which + "o", "T", "wfo", 4 * j, 4, ada=left)
    m = a = e = 0
    for r in runs:
        r["m0"], r["a0"], r["e0"] = m, a, e
        m += r["n"]
        a += r["n"] * r["ada"] // 2
        e += r["steps"]
    assert a == ADA_GROUPS
    return runs


RUNS = stream_plan()
RUN = {r["name"]: r for r in RUNS}

MOD_READS = [RUN["fci"]["a0"], RUN["kc"]["a0"], RUN["ao"]["a0"], ADA_GROUPS]


FILLS = ["n0", "p0", "m0", "g0", "n1", "p1", "m1", "g1",
         "nfc", "yfc", "nfx", "yfx", "nkc", "nx1", "ya", "nci", "yco", "nf3", "yf3"]
SPLITS = {n: i for i, n in enumerate(n for n in FILLS if n[0] != "n")}
NORMS = {n: i for i, n in enumerate(["n0", "n1", "fin", "nfc", "nfx", "nkc", "nx1", "nci", "nf3", "end"])}
U_NORMS = {n: i for i, n in enumerate(n for n in FILLS if n[0] == "n")}


def first_units(l):
    return ([("a", h, 0) for h in range(6)] + [("b", h, 0) for h in range(5)]
            + [("c", h, s) for h in range(5) for s in range(2)])


UNITS1 = first_units(0)
N1 = len(UNITS1)
UNITS2 = [("x", h, b) for h in range(32) for b in range(2)]
N2 = len(UNITS2)
HAS_T1 = [not (m == "c" and s == 0) for m, h, s in UNITS1]
NT1 = sum(HAS_T1)


def unit_numbers():
    flags = HAS_T1 + HAS_T1 + [True] * N2
    out, n = [], 0
    for f in flags:
        n += f
        out.append(n)
    return out


TN = unit_numbers()


def build(nc, w, vec, out):
    ctx = ExitStack()
    with ctx:
        base = 16512
        place = {}

        def sb(name, cols, dt=F32, at=None):
            nonlocal base
            if at is None:
                at = base
                base += (cols * 4 + 31) // 32 * 32
            place[name] = at
            return nc.alloc_sbuf_tensor_at(name, [P, cols], dt, offset=at)

        def sem(name):
            return ctx.enter_context(nc.semaphore(name))

        raw_t = sb("raw", SLABS * 2048)
        whi_t = sb("whi", 2 * 2048, F32R)
        wlo_t = sb("wlo", SLABS * 2048, F32R, at=place["raw"])
        aslab = sb("aslab", 2 * 1024)[:, :].rearrange("p (s k n) -> p s k n", s=2, k=2)
        acc_t = sb("acc", 2 * 512)
        asum_t = sb("asum", 2 * 512)
        h_t = sb("h", KT * T)
        uhi_t = sb("uhi", KT * T, F32R)
        ulo_t = sb("ulo", KT * T, F32R)
        kk = sb("kk", K_N)
        ones = sb("ones", P)
        cols = sb("cols", NCOL)
        sq = sb("sq", 2048)
        sc = sb("sc", 3 * 512)
        pt = sb("pt", 2 * 512)
        mod = sb("mod", 4 * 96)
        gs = sb("gs", 4 * 32)
        lamr = sb("lamr", 2 * 4 * 64)
        sinkr = sb("sinkr", 32)
        sm = sb("sm", 128)
        arena = base

        def tiles(t, n=T):
            return t[:, :].rearrange("p (k n) -> p k n", n=n)

        raw = tiles(raw_t, 2048)
        whi, wlo = tiles(whi_t, 2048), tiles(wlo_t, 2048)
        acc, asum = tiles(acc_t, 512), tiles(asum_t, 512)
        hh, uhi, ulo = tiles(h_t), tiles(uhi_t), tiles(ulo_t)
        scs, pts = tiles(sc, 512), tiles(pt, 512)
        tt4 = sc[:, 0:1024].rearrange("p (k n) -> p k n", n=T)
        mods = mod[:, :].rearrange("p (l c b) -> p l c b", l=4, c=2)

        zz_t = sb("zz", 48 * T)
        zz = tiles(zz_t)
        vv = sb("vv", 2 * V_COLS)[:, :].rearrange("p (t n) -> p t n", t=2)
        tabs_t = sb("tabs", 6 * T)
        tabs = tiles(tabs_t)
        praw = tiles(sb("praw", 2 * T, at=place["lamr"]))
        an_t = sb("an", 15 * T, at=place["uhi"])
        an = tiles(an_t)
        va_t = sb("va", 2 * 768, at=place["uhi"] + 15 * T * 4)
        va = va_t[:, :].rearrange("p (t n) -> p t n", t=2)
        cqh = tiles(sb("cqh", 5 * T, F32R, at=place["va"] + 2 * 768 * 4))
        cql = tiles(sb("cql", 5 * T, F32R, at=place["cqh"] + 5 * T * 4))
        assert place["cql"] + 5 * T * 4 <= place["uhi"] + 2 * KT * T * 4
        posi = sb("posi", T, I32, at=place["zz"])
        ang = sb("ang", 3 * T, at=place["zz"] + T * 4)
        trn = sb("trn", 3 * T, at=place["ang"] + 3 * T * 4)
        red = sb("red", 3 * T, at=place["trn"] + 3 * T * 4)

        cc_t = sb("cc", KT * T, at=arena)
        cc = tiles(cc_t)
        zf_t = sb("zf", KT * T, at=arena + 16384)
        zf = tiles(zf_t)
        ab = sb("ab", 2 * 1024, at=arena + 32768)[:, :].rearrange("p (s t n) -> p s t n", s=2, t=2)
        zq_t = sb("zq", 32 * T, at=arena)
        zq = tiles(zq_t)
        kx = tiles(sb("kx", 4 * T, at=arena + 32768))
        kc = tiles(sb("kc", 4 * T, at=arena + 36864))
        vx = tiles(sb("vx", 2 * T, at=arena + 40960))
        vc = tiles(sb("vc", 2 * T, at=arena + 43008))
        PADT = T + 30
        gp_t = sb("gp", KT * PADT, at=arena)
        gp = gp_t[:, :].rearrange("p (k n) -> p k n", n=PADT)
        zs_t = sb("zs", KT * T, at=arena + KT * PADT * 4)
        zs = tiles(zs_t)
        yc_t = sb("yc", KT * T, at=arena + KT * PADT * 4 + 16384)
        yc = tiles(yc_t)
        k2 = sb("k2", K2_N, at=arena + 52224)
        assert arena + 52224 + K2_N * 4 <= 229368 and base <= 229368, (base, arena)
        dft = k2[:, K2_DFT:K2_DFT + 1024].rearrange("p (k n) -> p k n", k=2)

        bank = [ctx.enter_context(nc.psum_tensor(f"bank{i}", [P, 512], F32)) for i in range(8)]

        ident = kk[:, K_ID:K_ID + P]
        mask1 = kk[:, K_MASK:K_MASK + 512]
        mask2 = k2[:, K2_MASK:K2_MASK + 1024].rearrange("p (b n) -> p b n", b=2)

        def rot(i):
            return kk[:, K_ROT + P * i:K_ROT + P * (i + 1)]

        def col(name, i, n=1):
            return cols[:, COL[name] + i:COL[name] + i + n]

        s_in = sem("inputs_loaded")
        s_x = sem("x_loaded")
        s_p = sem("ple_input_loaded")
        s_c = sem("context_loaded")
        s_const = sem("constants_set")
        s_raw = [sem(f"slab_loaded{i}") for i in range(SLABS)]
        s_hi = sem("slab_hi_ready")
        s_lo = sem("slab_lo_ready")
        s_hh = sem("conv_slab_first_half_hi_ready")
        s_slab = sem("slab_multiplied")
        s_ada = sem("ada_group_in_columns")
        s_araw = [sem(f"ada_half_slab_loaded{i}") for i in range(2)]
        s_acc = sem("ada_vector_steps")
        s_up = sem("lowrank_blocks_summed")
        s_drain = sem("projection_drained")
        s_gu = sem("gate_used")
        s_uh = sem("u_hi_ready")
        s_ul = sem("u_lo_ready")
        s_sq = sem("squares_ready")
        s_ss = sem("squares_summed")
        s_rt = sem("root_ready")
        s_nt = sem("normed_ready")
        s_nh = sem("normed_hi_ready")
        s_nl = sem("normed_lo_ready")
        s_csq = sem("lowrank_squares_ready")
        s_css = sem("lowrank_squares_summed")
        s_crt = sem("lowrank_root_ready")
        s_ct = sem("lowrank_normed_ready")
        s_ch = sem("lowrank_hi_ready")
        s_cl = sem("lowrank_lo_ready")
        s_rm = sem("rope_rotated")
        s_ro = sem("rope_done")
        s_gate = sem("gates_ready")
        s_im = sem("index_scores_ready")
        s_ir = sem("index_relu_ready")
        s_ia = sem("index_added")
        s_s = sem("scores_ready")
        s_sd = sem("scores_drained")
        s_m = sem("max_ready")
        s_e = sem("exp_ready")
        s_pr = sem("probs_ready")
        s_t = sem("probs_transposed")
        s_tc = sem("probs_copied")
        s_o = sem("heads_out_ready")
        s_of = sem("heads_out_used")
        s_osq = sem("subln_squares_ready")
        s_oss = sem("subln_squares_summed")
        s_ort = sem("subln_root_ready")
        s_mix = sem("mixed_ready")
        s_lam = sem("lambda_steps")
        s_sin = sem("table_angle_ready")
        s_tab = sem("tables_ready")
        s_mod = sem("modulation_ready")
        s_sil = sem("cond_silu_ready")
        s_f1 = sem("dft_tokens_ready")
        s_fa = sem("dft_tokens_copied")
        s_f2 = sem("dft_summed")
        s_fb = sem("dft_copied")
        s_cg = sem("conv_gates_ready")
        s_conv = sem("conv_done")
        s_cb = sem("conv_last_blocks_begun")
        s_lnq = sem("conv_squares_ready")
        s_lns = sem("conv_sums_ready")
        s_lnr = sem("conv_mean_off")
        s_lny = sem("conv_normed_ready")
        s_lnz = sem("conv_silu_ready")
        s_yd = sem("gated_ready")
        s_cvr = sem("conv_root_ready")
        s_yc = sem("conv_gated_ready")
        s_fin = sem("first_block_normed")
        s_out = sem("output_stored")
        s_dv = sem("vector_steps")

        INPUT_DMAS = 6

        def ada_at(a, both):
            return a * 32 if both else a * 17 + (32 - 17) * ADA_BOTH

        def ada_both(r, g0):
            return r["a0"] + g0 // 2 < ADA_BOTH

        def conv_squares(c):
            return (sq[:, 0:1024], sq[:, 1024:2048], pt[:, :], sq[:, 0:1024])[c]

        def squares(c):
            return (sq[:, 0:1024], sq[:, 1024:2048], sc[:, 0:1024], pt[:, :])[c]

        def rope_jobs():
            jobs = [(zz_t[:, T * b:T * (b + 2)], 1, 2) for b in range(Z_QB, Z_QB + 10, 2)]
            jobs += [(zz_t[:, T * b:T * min(b + 2, Z_QI + 15)], 2, min(2, Z_QI + 15 - b))
                     for b in range(Z_QI, Z_QI + 15, 2)]
            jobs += [(zz_t[:, T * Z_KR:T * (Z_KR + 1)], 0, 1)]
            jobs += [(an_t[:, T * 6:T * 8], 0, 2), (an_t[:, T * 8:T * 9], 0, 1)]
            return jobs

        NJ = 16
        NJX = 10

        def rope_jobs_x():
            jobs = [(kx[:, 2 * i:2 * i + 2, :].rearrange("p k n -> p (k n)"), 3, 2) for i in range(2)]
            return jobs + [(zq_t[:, T * 2 * i:T * 2 * (i + 1)], 3, 2) for i in range(8)]

        block = ctx.enter_context(nc.Block())

        @block.sync
        def _(sp):
            def load(r, g, s):
                src = w[r["w"]]
                if r["width"] == 2048:
                    sp.dma_start(raw[:, s, :], src[r["first"] + g, s]).then_inc(s_raw[s], 16)
                else:
                    sp.dma_start(raw[:, s, 0:r["width"]],
                                 src[r["first"] + g, s, :, 0:r["width"]]).then_inc(s_raw[s], 16)

            sp.wait_ge(s_in, 16 * INPUT_DMAS)
            for r in RUNS:
                for s in range(SLABS):
                    if r["m0"]:
                        sp.wait_ge(s_slab, SLABS * (r["m0"] - 1) + s + 1)
                    load(r, 0, s)
                if r["n"] > 1:
                    with sp.Fori(1, r["n"]) as g:
                        for s in range(SLABS):
                            sp.wait_ge(s_slab, g * SLABS + (SLABS * (r["m0"] - 1) + s + 1)
                                       if r["m0"] else g * SLABS + (s + 1) - SLABS)
                            load(r, g, s)
            for c in range(4):
                sp.wait_ge(s_yd, c + 1)
                sp.dma_start(out[:, 4 * c:4 * c + 4, :], zf[:, 4 * c:4 * c + 4, :]).then_inc(s_out, 16)
            sp.wait_ge(s_out, 64)

        @block.gpsimd
        def _(pool):
            nc.gpsimd.memset(ones[:, :], 1.0).then_inc(s_const, 1)

            def load(a, i, both):
                per = 4 if both else 2
                if i >= 2:
                    pool.wait_ge(s_acc, ada_at(a, both) + per * (i - 1))
                elif not isinstance(a, int) or a:
                    before = both or isinstance(a, int)
                    pool.wait_ge(s_acc, ada_at(a, both) - ((4 if before else 2) * (1 - i) + (not before)))
                pool.dma_start(aslab[:, i % 2, :, :].rearrange("p k n -> p (k n)"),
                               w["ada"][a, i // 2, :, 1024 * (i % 2):1024 * (i % 2) + 1024])\
                    .then_inc(s_araw[i % 2], 16)

            def group(a, both):
                for i in range(8):
                    load(a, i, both)
            group(0, True)
            with pool.Fori(1, ADA_BOTH) as a:
                group(a, True)
            group(ADA_BOTH, False)
            with pool.Fori(ADA_BOTH + 1, RUN["co"]["a0"]) as a:
                group(a, False)
            m0 = SLABS * RUN["ci"]["m0"]
            pool.wait_ge(s_lo, m0)
            with pool.Fori(0, 12) as g:
                for s in range(SLABS):
                    pool.wait_ge(s_hh, g * SLABS + (s + 1))
                    nc.gpsimd.tensor_tensor(wlo[:, s, 0:1024], raw[:, s, 0:1024],
                                            whi[:, s % 2, 0:1024].bitcast(F32), ALU.subtract)
                    pool.wait_ge(s_hi, g * SLABS + (m0 + s + 1))
                    nc.gpsimd.tensor_tensor(wlo[:, s, 1024:2048], raw[:, s, 1024:2048],
                                            whi[:, s % 2, 1024:2048].bitcast(F32),
                                            ALU.subtract).then_inc(s_lo, 1)
            with pool.Fori(RUN["co"]["a0"], ADA_GROUPS) as a:
                group(a, False)

        @block.tensor
        def _(pe):
            def filled(fill, s):
                if fill in NORMS:
                    return s_nl, 16 * U_NORMS[fill] + 4 * (s + 1)
                return s_ul, 4 * SPLITS[fill] + s + 1

            def mm3(o, whi_, wlo_, xhi_, xlo_, start, stop):
                nc.tensor.matmul(o, whi_, xhi_, start=start, stop=False, skip_group_check=True)
                nc.tensor.matmul(o, whi_, xlo_, start=False, stop=False, skip_group_check=True)
                return nc.tensor.matmul(o, wlo_, xhi_, start=False, stop=stop, skip_group_check=True)

            def step_banks(e):
                return (bank[2 * (e % 2)], bank[2 * (e % 2) + 1])

            def slab_t(s, par):
                for k in range(4):
                    kt = 4 * s + k
                    for b in range(4):
                        wc = slice(512 * k + P * b, 512 * k + P * (b + 1))
                        o = bank[2 * par + b // 2][:, T * (b % 2):T * (b % 2) + T]
                        last = mm3(o, whi[:, s % 2, wc], wlo[:, s, wc], uhi[:, kt, :], ulo[:, kt, :],
                                   kt == 0 and b % 2 == 0, kt == KT - 1)
                return last

            def slab_n(s, par, width):
                for k in range(4):
                    kt = 4 * s + k
                    for t in range(2):
                        tk = slice(P * t, P * (t + 1))
                        wc = slice(512 * k, 512 * k + width)
                        o = bank[2 * par + t][:, 0:width]
                        nc.tensor.matmul(o, uhi[:, kt, tk], whi[:, s % 2, wc], start=kt == 0,
                                         stop=False, skip_group_check=True)
                        nc.tensor.matmul(o, uhi[:, kt, tk], wlo[:, s, wc], start=False,
                                         stop=False, skip_group_check=True)
                        last = nc.tensor.matmul(o, ulo[:, kt, tk], whi[:, s % 2, wc], start=False,
                                                stop=kt == KT - 1, skip_group_check=True)
                return last

            def group(r, g, par, slab, fill=None):
                e = g + r["e0"]
                if not (isinstance(e, int) and e < 2):
                    pe.wait_ge(s_drain, (e - 1) * 2)
                for s in range(SLABS):
                    if fill is not None:
                        pe.wait_ge(*filled(fill, s))
                    pe.wait_ge(s_lo, (g + r["m0"]) * SLABS + (s + 1))
                    last = slab(s, par)
                    last.then_inc(s_slab, 1)

            def project(name, fill, width=512, g0=0, n=None):
                r = RUN[name]
                n = r["n"] if n is None else n
                slab = slab_t if r["kind"] == "T" else (lambda s, par: slab_n(s, par, width))
                both = ada_both(r, g0)

                def ada_after(g, pair, second):
                    if r["ada"] == 2:
                        ada(g + r["a0"], both)
                    elif r["ada"] and second:
                        ada(pair + r["a0"], both)
                for g in range(g0, g0 + min(n, 2)):
                    group(r, g, (r["e0"] + g) % 2, slab, fill if g == g0 else None)
                    ada_after(g, g // 2, g % 2)
                if n > 2:
                    with pe.Fori(g0 // 2 + 1, (g0 + n) // 2) as j:
                        for half in range(2):
                            group(r, j * 2 + half, (r["e0"] + half) % 2, slab)
                            ada_after(j * 2 + half, j, half)

            def ada(a, both):
                for layer, reads in enumerate(MOD_READS):
                    if isinstance(a, int) and a == reads:
                        pe.wait_ge(s_mod, layer + 1)
                pe.wait_ge(s_acc, ada_at(a, both) + (32 if both else 17))
                for c in range(1 + both):
                    for b in range(4):
                        at = 4 * ADA_GROUPS * c + b
                        o = bank[4][:, 4 * a + at:4 * a + at + 1] if isinstance(a, int) \
                            else bank[4][:, bass.ds(a * 4 + at, 1)]
                        last = nc.tensor.matmul(o, asum[:, c, P * b:P * (b + 1)], ones[:, 0:1],
                                                start=True, stop=True, skip_group_check=True)
                last.then_inc(s_ada, 1)

            def norm(name):
                n = NORMS[name]
                for c in range(4):
                    pe.wait_ge(s_sq, 4 * n + c + 1)
                    for k in range(4):
                        last = nc.tensor.matmul(bank[7][:, 0:T], ones[:, :],
                                                squares(c)[:, T * k:T * (k + 1)],
                                                start=c == 0 and k == 0, stop=c == 3 and k == 3)
                    last.then_inc(s_ss, 1)

            def rope(jobs, base_job, i):
                x, kind, nb = jobs[i]
                if i >= 3:
                    pe.wait_ge(s_ro, base_job + i - 2)
                nc.tensor.matmul(bank[5 + i % 3][:, 0:T * nb], rot(kind), x,
                                 start=True, stop=True).then_inc(s_rm, 1)

            def softmax_units(first, n, scores, transposes, values):
                for t in range(n + 3):
                    if t < n:
                        u = first + t
                        if t >= 2:
                            pe.wait_ge(s_sd, u - 1)
                        scores(t, bank[t % 2]).then_inc(s_s, 1)
                    if 2 <= t < n + 2:
                        i = t - 2
                        tn = TN[first + i]
                        if transposes(i, None, None):
                            pe.wait_ge(s_pr, first + i + 1)
                            if i >= 2:
                                pe.wait_ge(s_tc, tn - 2)
                            transposes(i, bank[2 + tn % 2], scs[:, i % 3, :]).then_inc(s_t, 1)
                    if t >= 3:
                        i = t - 3
                        tn = TN[first + i]
                        if transposes(i, None, None):
                            pe.wait_ge(s_tc, tn)
                            values(i, pts[:, tn % 2, :]).then_inc(s_o, 1)

            def first_block(l):
                norm(f"n{l}")
                project(f"in{l}", f"n{l}")
                r = RUN[f"v{l}"]
                for g in range(3):
                    group(r, g, (r["e0"] + g) % 2,
                          lambda s, par, n=512 if g < 2 else V_COLS - 1024: slab_n(s, par, n))
                    if g == 1:
                        ada(r["a0"], True)
                jobs = rope_jobs()
                pe.wait_ge(s_drain, 2 * (RUN[f"v{l}"]["e0"] + 3))
                pe.wait_ge(s_csq, l + 1)
                for k in range(5):
                    last = nc.tensor.matmul(bank[7][:, T * (k > 2):T * (k > 2) + T], ones[:, :],
                                            sq[:, T * k:T * (k + 1)], start=k in (0, 3), stop=k in (2, 4),
                                            skip_group_check=True)
                last.then_inc(s_css, 1)
                up(l, jobs)
                pe.wait_ge(s_drain, 2 * (RUN[f"up{l}"]["e0"] + 6))
                for i in (14, 15):
                    rope(jobs, NJ * l, i)
                pe.wait_ge(s_ro, NJ * l + 16)
                for h in range(8):
                    if h >= 2:
                        pe.wait_ge(s_ir, 8 * l + h - 1)
                    rows = slice(64 * (h % 2), 64 * (h % 2) + 64)
                    for t in range(2):
                        last = nc.tensor.matmul(bank[5 + h % 2][:, T * t:T * (t + 1)],
                                                zz[rows, Z_QI + h // 2, P * t:P * (t + 1)],
                                                zz[rows, Z_KI, :], start=True, stop=True,
                                                skip_group_check=True)
                    last.then_inc(s_im, 1)

                def scores(i, ps):
                    m, h, part = UNITS1[i]
                    for t in range(2):
                        o = ps[:, T * t:T * (t + 1)]
                        tk = slice(P * t, P * (t + 1))
                        if m == "a":
                            rows = slice(64 * (h % 2), 64 * (h % 2) + 64)
                            nc.tensor.matmul(o, an[:, h, tk], an[:, AN_KN + h, :], start=True,
                                             stop=False, skip_group_check=True)
                            last = nc.tensor.matmul(o, an[rows, AN_QR + h // 2, tk], zz[rows, Z_KR, :],
                                                    start=False, stop=True, skip_group_check=True)
                        elif m == "b":
                            last = nc.tensor.matmul(o, zz[:, Z_QB + h, tk], zz[:, Z_KB + h, :],
                                                    start=True, stop=True, skip_group_check=True)
                        else:
                            rows = slice(64 * part, 64 * part + 64)
                            last = nc.tensor.matmul(o, zz[rows, Z_QC + h, tk], zz[rows, Z_KC + h, :],
                                                    start=True, stop=True, skip_group_check=True)
                    return last

                def transposes(i, ps, pr):
                    if ps is None:
                        return HAS_T1[i]
                    for n, c in enumerate((0, 2, 3)):
                        last = nc.tensor.transpose(ps[:, P * n:P * (n + 1)], pr[:, P * c:P * (c + 1)], ident)
                    return last

                def values(i, p):
                    m, h, part = UNITS1[i]
                    tn = TN[N1 * l + i] - 1
                    if tn >= 2:
                        pe.wait_ge(s_of, tn - 1)
                    o = bank[5 + tn % 2]
                    if m == "a":
                        v = [va[:, k, P * h:P * (h + 1)] for k in range(2)]
                    else:
                        at = (V_B if m == "b" else V_C) + P * h
                        v = [vv[:, k, at:at + P] for k in range(2)]
                    nc.tensor.matmul(o[:, 0:P], v[0], p[:, 0:P], start=True, stop=True,
                                     skip_group_check=True)
                    nc.tensor.matmul(o[:, P:T], v[0], p[:, P:2 * P], start=True, stop=False,
                                     skip_group_check=True)
                    return nc.tensor.matmul(o[:, P:T], v[1], p[:, 2 * P:3 * P], start=False, stop=True,
                                            skip_group_check=True)

                pe.wait_ge(s_ir, 8 * l + 8)
                softmax_units(N1 * l, N1, scores, transposes, values)
                pe.wait_ge(s_osq, l + 1)
                for c in range(3):
                    n = 512 if c < 2 else 256
                    last = nc.tensor.matmul(bank[5 + c][:, 0:n], ones[:, :], sq[:, 512 * c:512 * c + n],
                                            start=True, stop=True)
                last.then_inc(s_oss, 1)
                r = RUN[f"ple{l}"]
                pe.wait_ge(s_ul, 4 * SPLITS[f"p{l}"] + 4)
                for s in range(SLABS):
                    pe.wait_ge(s_drain, 2 * (r["e0"] + s - 1))
                    pe.wait_ge(s_lo, SLABS * r["m0"] + s + 1)
                    b0, b1 = step_banks(r["e0"] + s)
                    for k in range(2):
                        for b in range(4):
                            wc = slice(512 * k + P * b, 512 * k + P * (b + 1))
                            o = (b0, b1)[b // 2][:, T * (b % 2):T * (b % 2) + T]
                            last = mm3(o, whi[:, s % 2, wc], wlo[:, s, wc], uhi[:, k, :], ulo[:, k, :],
                                       k == 0 and b % 2 == 0, k == 1)
                    last.then_inc(s_slab, 1)
                project(f"o{l}", f"m{l}")
                project(f"pg{l}", f"g{l}")

            def up(l, jobs):
                r = RUN[f"up{l}"]
                pe.wait_ge(s_cl, l + 1)
                slab = [-1]

                def need(s):
                    if s > slab[0]:
                        pe.wait_ge(s_lo, SLABS * r["m0"] + s + 1)
                        slab[0] = s

                tile = 0
                for b in range(15):
                    e = r["e0"] + b // 4
                    o = step_banks(e)[(b % 4) // 2][:, T * (b % 2):T * (b % 2) + T]
                    if b < 14:
                        rope(jobs, NJ * l, b)
                    if b % 4 == 0:
                        pe.wait_ge(s_drain, 2 * (e - 1))
                    nk, k0 = (3, 0) if b < 9 else (2, 3)
                    if b == 5:
                        tile = 16
                    for k in range(nk):
                        s = tile // 16
                        need(s)
                        wc = slice(P * (tile % 16), P * (tile % 16 + 1))
                        last = mm3(o, whi[:, s % 2, wc], wlo[:, s, wc], cqh[:, k0 + k, :],
                                   cql[:, k0 + k, :], k == 0 and b % 2 == 0, k == nk - 1)
                        tile += 1
                    if b in (4, 10):
                        last.then_inc(s_slab, 1)
                    if b in (3, 7, 11, 14):
                        last.then_inc(s_up, 1)
                for part, (s, c0, n) in enumerate(((2, 1024, 512), (3, 0, 256))):
                    e = r["e0"] + 4 + part
                    pe.wait_ge(s_drain, 2 * (e - 1))
                    need(s)
                    for t in range(2):
                        tk = slice(P * t, P * (t + 1))
                        o = step_banks(e)[t][:, 0:n]
                        for k in range(2):
                            wc = slice(c0 + n * k, c0 + n * (k + 1))
                            nc.tensor.matmul(o, cqh[:, 3 + k, tk], whi[:, s % 2, wc], start=k == 0,
                                             stop=False, skip_group_check=True)
                            nc.tensor.matmul(o, cqh[:, 3 + k, tk], wlo[:, s, wc], start=False,
                                             stop=False, skip_group_check=True)
                            last = nc.tensor.matmul(o, cql[:, 3 + k, tk], whi[:, s % 2, wc], start=False,
                                                    stop=k == 1, skip_group_check=True)
                    last.then_inc(s_slab, 1)

            def fourier(tag, n_inv):
                norm("nf" + tag)
                r = RUN[f"f{tag}i"]
                project(f"f{tag}i", f"nf{tag}", n=4)
                for g in range(8):
                    for t in range(2):
                        if g == 0 and t == 0:
                            pe.wait_ge(s_drain, 2 * (r["e0"] + 4))
                        i = 16 * n_inv + 2 * g + t
                        if i >= 2:
                            pe.wait_ge(s_fa, i - 1)
                        for k in range(2):
                            last = nc.tensor.matmul(bank[5 + t][:, :], zf[:, 2 * g + k, P * t:P * (t + 1)],
                                                    dft[:, k, :], start=k == 0, stop=k == 1)
                        last.then_inc(s_f1, 1)
                    pe.wait_ge(s_fa, 16 * n_inv + 2 * g + 2)
                    if 8 * n_inv + g >= 1:
                        pe.wait_ge(s_fb, 8 * n_inv + g)
                    for b in range(2):
                        n = 0
                        for cs in range(2):
                            for k in range(2):
                                last = nc.tensor.matmul(bank[7][:, T * b:T * (b + 1)],
                                                        ab[:, g % 2, k, T * cs + P * b:T * cs + P * (b + 1)],
                                                        dft[:, k, T * cs:T * (cs + 1)],
                                                        start=n == 0, stop=n == 3, skip_group_check=True)
                                n += 1
                    last.then_inc(s_f2, 1)
                project(f"f{tag}i", None, g0=4, n=4)
                project(f"f{tag}o", f"yf{tag}")

            pe.wait_ge(s_const, 1)
            pe.wait_ge(s_in, 16 * INPUT_DMAS)
            for l in range(2):
                first_block(l)
            norm("fin")
            pe.wait_ge(s_c, 32)
            fourier("c", 0)
            fourier("x", 1)
            norm("nkc")
            project("kc", "nkc")
            project("vc", None, 256)
            norm("nx1")
            project("kx", "nx1")
            project("vx", None, 256)
            project("qz", None)
            pe.wait_ge(s_drain, 2 * (RUN["qz"]["e0"] + 8))
            for i in range(NJX):
                rope(rope_jobs_x(), 2 * NJ, i)
            pe.wait_ge(s_ro, 2 * NJ + NJX)

            def scores(i, ps):
                _, h, b = UNITS2[i]
                rows = slice(64 * (h % 2), 64 * (h % 2) + 64)
                q = zq[rows, h // 2, P * b:P * (b + 1)]
                nc.tensor.matmul(ps[:, 0:T], q, kx[rows, h // 8, :], start=True, stop=True,
                                 skip_group_check=True)
                return nc.tensor.matmul(ps[:, T:2 * T], q, kc[rows, h // 8, :], start=True, stop=True,
                                        skip_group_check=True)

            def transposes(i, ps, pr):
                if ps is None:
                    return True
                for c in range(4):
                    last = nc.tensor.transpose(ps[:, P * c:P * (c + 1)], pr[:, P * c:P * (c + 1)], ident)
                return last

            def values(i, p):
                _, h, b = UNITS2[i]
                if h % 2 == 0 and b == 0:
                    pe.wait_ge(s_of, 2 * NT1 + max(0, h // 2 - 1))
                o = bank[5 + (h // 2) % 2][64 * (h % 2):64 * (h % 2) + 64, P * b:P * (b + 1)]
                for c in range(4):
                    v = (vx if c < 2 else vc)[:, c % 2, 64 * (h // 8):64 * (h // 8) + 64]
                    last = nc.tensor.matmul(o, v, p[:, P * c:P * (c + 1)], start=c == 0, stop=c == 3,
                                            skip_group_check=True)
                return last

            softmax_units(2 * N1, N2, scores, transposes, values)
            project("ao", "ya")
            norm("nci")
            project("ci", "nci", n=10)
            project("ci", None, g0=10, n=1)
            for c in range(4):
                pe.wait_ge(s_conv, 4 * c + 4)
                for k in range(4):
                    last = nc.tensor.matmul(bank[5][:, 0:T], ones[:, :], yc[:, 4 * c + k, :],
                                            start=c == 0 and k == 0, stop=c == 3 and k == 3)
            last.then_inc(s_lns, 1)
            project("ci", None, g0=11, n=1)
            for c in range(4):
                pe.wait_ge(s_lnq, c + 1)
                for k in range(4):
                    last = nc.tensor.matmul(bank[6][:, 0:T], ones[:, :],
                                            conv_squares(c)[:, T * k:T * (k + 1)],
                                            start=c == 0 and k == 0, stop=c == 3 and k == 3)
                last.then_inc(s_lns, 1)
            project("co", "yco")
            fourier("3", 2)
            norm("end")

        NORM_ARGS = {
            "n0": (hh, "in", None), "n1": (hh, "pg0", None), "nfc": (cc, "c", (0, 1)),
            "fin": (hh, "pg1", None), "nfx": (hh, "fin", (0, 0)), "nkc": (cc, "fco", (1, 1)), "nx1": (hh, "fxo", (1, 0)),
            "nci": (hh, "ao", (2, 0)), "nf3": (hh, "co", (3, 0)), "end": (hh, "f3o", None),
        }
        GATED = {"pg0": 0, "pg1": 4, "fc": 8, "fx": 12, "f3": 16}
        SM_NM, SM_SUM, SM_RI, SM_RL, SM_SIL, SM_LAM, SM_SUBG, SM_TMP, SM_M8, SM_ES = (
            0, 8, 16, 24, 32, 64, 66, 68, 80, 96)

        AFTER_NORM = {"n0": "in0", "n1": "in1", "nfc": "fci", "nfx": "fxi", "nkc": "kc", "nx1": "kx",
                      "nci": "ci", "nf3": "f3i"}

        def source_ready(eng, name, chunk=3):
            src = NORM_ARGS[name][1]
            if src == "in":
                eng.wait_ge(s_x, 64)
            elif src == "c":
                eng.wait_ge(s_c, 32)
            elif src == "fin":
                eng.wait_ge(s_fin, chunk + 1)
            elif src.startswith("pg"):
                eng.wait_ge(s_gu, 4 * int(src[2]) + max(chunk + 1, 3 + min(chunk, 1)))
            else:
                eng.wait_ge(s_drain, 2 * (RUN[src]["e0"] + chunk + 1))

        def norm_scale(name, kt):
            if name in ("n0", "n1"):
                return col("norm_g", 16 * int(name[1]) + kt)
            if name == "end":
                return col("final_g_2", kt)
            if name == "fin":
                return col("final_g", kt)
            l, c = NORM_ARGS[name][2]
            return gs[:, 32 * l + 16 * c + kt:32 * l + 16 * c + kt + 1]

        def norm_shift(name, kt):
            if NORM_ARGS[name][2] is None:
                return None
            l, c = NORM_ARGS[name][2]
            return mods[:, l, c, kt:kt + 1]

        @block.scalar
        def _(act):
            def split(r, g, s):
                act.wait_ge(s_raw[s], (g + (r["m0"] + 1)) * 16)
                n = r["width"]
                m = g * SLABS + (SLABS * r["m0"] + s)
                if not (isinstance(m, int) and m < 2):
                    act.wait_ge(s_slab, m - 1)
                if r["name"] == "ci":
                    nc.scalar.copy(whi[:, s % 2, 0:n // 2], raw[:, s, 0:n // 2]).then_inc(s_hh, 1)
                    nc.scalar.copy(whi[:, s % 2, n // 2:n], raw[:, s, n // 2:n]).then_inc(s_hi, 1)
                else:
                    nc.scalar.copy(whi[:, s % 2, 0:n], raw[:, s, 0:n]).then_inc(s_hi, 1)

            def presplit(name, g=0):
                split(RUN[name], g, 0)
                split(RUN[name], g, 1)

            def summed(r, g):
                act.wait_ge(s_slab, (g + (r["m0"] + 1)) * SLABS)

            def run(r, drain, g0=0, n=None, then=None, early=None):
                n = r["n"] if n is None else n
                split(r, g0, 2)
                split(r, g0, 3)

                def body(g, par):
                    split(r, g, 0)
                    split(r, g, 1)
                    drain(r, g - 1, par)
                    split(r, g, 2)
                    split(r, g, 3)
                pairs = (n - 1) // 2
                if pairs > 1:
                    with act.Fori(0, pairs) as j:
                        for half in range(2):
                            body(j * 2 + (g0 + 1 + half), (r["e0"] + g0 + half) % 2)
                else:
                    for g in range(1, 1 + 2 * pairs):
                        body(g0 + g, (r["e0"] + g0 + g - 1) % 2)
                if (n - 1) % 2:
                    body(g0 + n - 1, (r["e0"] + g0 + n - 2) % 2)
                if then is not None:
                    presplit(*then)
                if early is not None:
                    split(RUN[early], 0, 0)
                drain(r, g0 + n - 1, (r["e0"] + g0 + n - 1) % 2)

            def nothing(r, g, par):
                pass

            def copier(dest, func=ACT.Copy):
                def drain(r, g, par):
                    summed(r, g)
                    for half in range(2):
                        last = nc.scalar.activation(dest(g, half), bank[2 * par + half][:, :], func)
                    last.then_inc(s_drain, 2)
                return drain

            def gater(first, func, g0):
                def drain(r, g, par):
                    i = first + g - g0
                    if i >= 2:
                        act.wait_ge(s_gu, i - 1)
                    summed(r, g)
                    for half in range(2):
                        at = 1024 * (i % 2) + 512 * half
                        last = nc.scalar.activation(sq[:, at:at + 512], bank[2 * par + half][:, :], func)
                    last.then_inc(s_drain, 2)
                return drain

            def norm(name):
                n = NORMS[name]
                src = NORM_ARGS[name][0]
                if n:
                    act.wait_ge(s_ss, 4 * n)
                for c in range(4):
                    source_ready(act, name, c)
                    nc.scalar.activation(squares(c),
                                         src[:, 4 * c:4 * c + 4, :].rearrange("p k n -> p (k n)"),
                                         ACT.Square).then_inc(s_sq, 1)
                if name in AFTER_NORM:
                    split(RUN[AFTER_NORM[name]], 0, 1)
                act.wait_ge(s_ss, 4 * n + 4)
                if name == "nfc":
                    act.wait_ge(s_fin, 4)
                nc.scalar.activation(sc[:, 1024:1024 + T], bank[7][:, 0:T], ACT.Sqrt, bias=EPSB,
                                     scale=1.0 / D).then_inc(s_rt, 1)
                if name in ("fin", "end"):
                    return
                for kt in range(KT):
                    act.wait_ge(s_nt, 16 * U_NORMS[name] + kt + 1)
                    sh = norm_shift(name, kt)
                    if sh is None:
                        nc.scalar.copy(uhi[:, kt, :], tt4[:, kt % 4, :]).then_inc(s_nh, 1)
                    else:
                        nc.scalar.activation(uhi[:, kt, :], tt4[:, kt % 4, :], ACT.Identity,
                                             bias=sh).then_inc(s_nh, 1)

            def fill_u(name, src, next_run, chunks=4, width=1024, ready=None):
                act.wait_ge(s_slab, SLABS * RUN[next_run]["m0"])
                for c in range(chunks):
                    if ready is not None:
                        act.wait_ge(*ready(c))
                    nc.scalar.copy(uhi_t[:, width * c:width * (c + 1)],
                                   src[:, width * c:width * (c + 1)]).then_inc(s_uh, 1)

            EPSB = sm[:, 100:101]

            def softmax_units(first, n, exps, transposed):
                for t in range(n + 2):
                    if t < n:
                        u = first + t
                        act.wait_ge(s_m, u + 1)
                        exps(t).then_inc(s_e, 1)
                    if t >= 2:
                        i = t - 2
                        if not transposed(i):
                            continue
                        tn = TN[first + i]
                        act.wait_ge(s_t, tn)
                        if tn > 2:
                            act.wait_ge(s_o, tn - 2)
                        width = 3 * P if first < 2 * N1 else 4 * P
                        nc.scalar.copy(pts[:, tn % 2, 0:width], bank[2 + tn % 2][:, 0:width])\
                            .then_inc(s_tc, 1)

            act.dma_start(kk[:, :], vec["consts"]).then_inc(s_in, 16)
            act.dma_start(cols[:, :], vec["cols"]).then_inc(s_in, 16)
            act.dma_start(lamr[:, :], vec["lam"]).then_inc(s_in, 16)
            act.dma_start(sinkr[:, :], vec["sink"]).then_inc(s_in, 16)
            act.dma_start(posi[:, :], vec["pos"]).then_inc(s_in, 16)
            act.dma_start(sm[:, 100:101], vec["eps"]).then_inc(s_in, 16)
            for c in range(4):
                act.dma_start(hh[:, 4 * c:4 * c + 4, :], vec["x"][:, 4 * c:4 * c + 4, :]).then_inc(s_x, 16)
            act.wait_ge(s_in, 16 * INPUT_DMAS)
            nc.scalar.activation(sm[:, SM_SIL:SM_SIL + 32:2], col("c_2", 0, 16), ACT.Silu)
            nc.scalar.activation(sm[:, SM_SIL + 1:SM_SIL + 32:2], col("c_ctx_2", 0, 16), ACT.Silu)\
                .then_inc(s_sil, 1)
            act.wait_ge(s_lam, 1)
            act.dma_start(praw[:, :, :], vec["p"][0]).then_inc(s_p, 16)
            nc.scalar.activation(sm[:, SM_TMP + 4:SM_TMP + 8], sm[:, SM_TMP:SM_TMP + 4], ACT.Exp)\
                .then_inc(s_lam, 1)
            for i in range(2):
                act.wait_ge(s_sin, i + 1)
                nc.scalar.activation(tabs[:, i::2, :], red[:, :].rearrange("p (k n) -> p k n", n=T),
                                     ACT.Sin).then_inc(s_tab, 1)

            def first_block(l):
                if l == 0:
                    split(RUN["in0"], 0, 0)
                norm(f"n{l}")
                run(RUN[f"in{l}"], copier(lambda g, half: zz_t[:, bass.ds(g * 1024 + 512 * half, 512)]
                                          if not isinstance(g, int) else
                                          zz_t[:, 1024 * g + 512 * half:1024 * g + 512 * half + 512]),
                    then=(f"v{l}",))

                def drain_v(r, g, par):
                    summed(r, g)
                    n = 512 if g < 2 else V_COLS - 1024
                    for t in range(2):
                        last = nc.scalar.copy(vv[:, t, 512 * g:512 * g + n], bank[2 * par + t][:, 0:n])
                    last.then_inc(s_drain, 2)
                run(RUN[f"v{l}"], drain_v)
                act.wait_ge(s_drain, 2 * (RUN[f"v{l}"]["e0"] + 3))
                nc.scalar.activation(sq[:, 0:5 * T], zz_t[:, T * Z_CQ:T * (Z_CQ + 5)], ACT.Square)\
                    .then_inc(s_csq, 1)
                act.wait_ge(s_css, l + 1)
                nc.scalar.activation(sc[:, 0:T], bank[7][:, 0:T], ACT.Sqrt, bias=EPSB, scale=1.0 / 384)
                nc.scalar.activation(sc[:, T:2 * T], bank[7][:, T:2 * T], ACT.Sqrt, bias=EPSB,
                                     scale=1.0 / 256).then_inc(s_crt, 1)
                act.wait_ge(s_ct, l + 1)
                nc.scalar.copy(cqh[:, :, :], sq[:, 0:5 * T].rearrange("p (k n) -> p k n", n=T))\
                    .then_inc(s_ch, 1)
                r = RUN[f"up{l}"]
                presplit(f"up{l}")
                split(r, 0, 2)

                def drain_up(i):
                    e = r["e0"] + i
                    par = e % 2
                    if i < 4:
                        act.wait_ge(s_up, 4 * l + i + 1)
                        for half in range(2):
                            n = 512 if (i, half) != (3, 1) else 256
                            at = 1024 * i + 512 * half
                            last = nc.scalar.copy(an_t[:, at:at + n], bank[2 * par + half][:, 0:n])
                    else:
                        act.wait_ge(s_slab, SLABS * r["m0"] + i - 1)
                        n, at = (512, 0) if i == 4 else (256, 512)
                        for t in range(2):
                            last = nc.scalar.copy(va[:, t, at:at + n], bank[2 * par + t][:, 0:n])
                    last.then_inc(s_drain, 2)
                drain_up(0)
                drain_up(1)
                split(r, 0, 3)
                nc.scalar.activation(zz_t[:, 0:16 * T], zz_t[:, 0:16 * T], ACT.Silu).then_inc(s_gate, 1)
                for i in range(2, 6):
                    drain_up(i)
                for h in range(8):
                    act.wait_ge(s_im, 8 * l + h + 1)
                    if h >= 2:
                        act.wait_ge(s_ia, 16 * l + 2 * (h - 1))
                    nc.scalar.activation(pts[:, h % 2, :], bank[5 + h % 2][:, :], ACT.Relu)\
                        .then_inc(s_ir, 1)

                def exps(i):
                    for t in range(2):
                        x = scs[:, i % 3, T * t:T * (t + 1)]
                        c = 2 * (i % 4) + t
                        last = nc.scalar.activation(x, x, ACT.Exp, bias=sm[:, SM_NM + c:SM_NM + c + 1],
                                                    accum_out=sm[:, SM_SUM + c:SM_SUM + c + 1])
                    return last
                softmax_units(N1 * l, N1, exps, lambda i: HAS_T1[i])
                act.wait_ge(s_of, NT1 * (l + 1))
                nc.scalar.activation(sq[:, 0:5 * T], zz_t[:, T * Z_CQ:T * (Z_CQ + 5)], ACT.Square)\
                    .then_inc(s_osq, 1)
                r = RUN[f"ple{l}"]
                presplit(f"ple{l}")
                act.wait_ge(s_p, 16 * (l + 1))
                nc.scalar.copy(uhi[:, 0:2, :], praw[:, :, :]).then_inc(s_uh, 4)
                act.wait_ge(s_oss, l + 1)
                for c in range(3):
                    n = 512 if c < 2 else 256
                    last = nc.scalar.activation(sc[:, 512 * c:512 * c + n], bank[5 + c][:, 0:n], ACT.Sqrt,
                                                bias=EPSB, scale=1.0 / P)
                last.then_inc(s_ort, 1)
                def drain_e(s):
                    act.wait_ge(s_slab, SLABS * r["m0"] + s + 1)
                    par = (r["e0"] + s) % 2
                    for half in range(2):
                        at = T * 16 + 1024 * s + 512 * half
                        last = nc.scalar.copy(zz_t[:, at:at + 512], bank[2 * par + half][:, :])
                    last.then_inc(s_drain, 2)
                for s in range(SLABS):
                    if s + 2 < SLABS:
                        split(r, 0, s + 2)
                    elif s == 2:
                        presplit(f"o{l}")
                    drain_e(s)
                act.wait_ge(s_mix, l + 1)
                fill_u(f"m{l}", zz_t, f"o{l}")
                run(RUN[f"o{l}"], nothing, then=(f"pg{l}",))
                if l == 0:
                    act.wait_ge(s_ul, 4 * SPLITS["p0"] + 4)
                    act.dma_start(praw[:, :, :], vec["p"][1]).then_inc(s_p, 16)
                fill_u(f"g{l}", h_t, f"pg{l}", ready=lambda c: (s_drain, 2 * (RUN[f"o{l}"]["e0"] + c + 1)))
                run(RUN[f"pg{l}"], gater(GATED[f"pg{l}"], ACT.Sigmoid, 0), early=("in1", "fci")[l])

            def fourier(tag, inv):
                r = RUN[f"f{tag}i"]
                norm("nf" + tag)
                run(r, copier(lambda g, half: zf_t[:, 1024 * g + 512 * half:1024 * g + 512 * half + 512]),
                    0, 4, then=(f"f{tag}i", 4))
                for g in range(8):
                    for t in range(2):
                        i = 16 * inv + 2 * g + t
                        act.wait_ge(s_f1, i + 1)
                        if 8 * inv + g >= 2:
                            act.wait_ge(s_f2, 8 * inv + g - 1)
                        nc.scalar.copy(ab[:, g % 2, t, 0:T], bank[5 + t][:, 0:T])
                        nc.scalar.activation(ab[:, g % 2, t, T:2 * T], bank[5 + t][:, T:2 * T], ACT.Copy,
                                             scale=-1.0).then_inc(s_fa, 1)
                run(r, gater(GATED["f" + tag], ACT.Silu, 4), 4, 4, then=(f"f{tag}o",))
                fill_u("yf" + tag, zf_t, f"f{tag}o", ready=lambda c: (s_gu, GATED["f" + tag] + c + 1))
                run(RUN[f"f{tag}o"], nothing, early={"c": "fxi", "x": "kc"}.get(tag))

            for l in range(2):
                first_block(l)
            act.wait_ge(s_gu, 8)
            act.dma_start(cc[:, :, :], vec["ctx"]).then_inc(s_c, 16)
            act.dma_start(k2[:, :], vec["consts2"]).then_inc(s_c, 16)
            norm("fin")
            fourier("c", 0)
            fourier("x", 1)
            norm("nkc")

            def flat(t, n):
                return lambda g, half: t[:, 2 * half:2 * half + 2, :].rearrange("p k n -> p (k n)")

            def drain_vx(dest):
                def drain(r, g, par):
                    summed(r, g)
                    for t in range(2):
                        last = nc.scalar.copy(dest[:, t, :], bank[2 * par + t][:, 0:T])
                    last.then_inc(s_drain, 2)
                return drain
            run(RUN["kc"], copier(flat(kc, 4)), then=("vc",))
            run(RUN["vc"], drain_vx(vc), early="kx")
            norm("nx1")
            run(RUN["kx"], copier(flat(kx, 4)), then=("vx",))
            run(RUN["vx"], drain_vx(vx), then=("qz",))
            run(RUN["qz"], copier(lambda g, half: zq_t[:, bass.ds(g * 1024 + 512 * half, 512)]
                                  if not isinstance(g, int) else
                                  zq_t[:, 1024 * g + 512 * half:1024 * g + 512 * half + 512]))
            act.wait_ge(s_drain, 2 * (RUN["qz"]["e0"] + 8))
            nc.scalar.activation(zq_t[:, 16 * T:32 * T], zq_t[:, 16 * T:32 * T], ACT.Silu)\
                .then_inc(s_gate, 1)

            def exps(i):
                _, h, b = UNITS2[i]
                x = scs[:, i % 3, :]
                c = 2 * (i % 4)
                nc.scalar.activation(x, x, ACT.Exp, bias=sm[:, SM_NM + c:SM_NM + c + 1],
                                     accum_out=sm[:, SM_SUM + c:SM_SUM + c + 1])
                return nc.scalar.activation(sm[:, SM_ES + i % 4:SM_ES + i % 4 + 1], sinkr[:, h:h + 1],
                                            ACT.Exp, bias=sm[:, SM_NM + c:SM_NM + c + 1])
            softmax_units(2 * N1, N2, exps, lambda i: True)
            presplit("ao")
            act.wait_ge(s_of, 2 * NT1 + 16)
            fill_u("ya", zq_t[:, 16 * T:32 * T], "ao")
            run(RUN["ao"], nothing, early="ci")
            norm("nci")
            r = RUN["ci"]

            def drain_ci(r, g, par):
                summed(r, g)
                if g < 8:
                    if g >= 2:
                        act.wait_ge(s_drain, 2 * (r["e0"] + g - 1))
                    nc.scalar.activation(sq[:, 1024 * (g % 2):1024 * (g % 2) + 512],
                                         bank[2 * par + 1][:, :], ACT.Sigmoid).then_inc(s_cg, 1)
                else:
                    if g == 8:
                        act.wait_ge(s_cb, 1)
                    for half in range(2):
                        at = 1024 * (g - 8) + 512 * half
                        last = nc.scalar.activation(zs_t[:, at:at + 512], bank[2 * par + half][:, :],
                                                    ACT.Silu)
                    last.then_inc(s_drain, 2)
            split(r, 0, 2)
            split(r, 0, 3)
            for g in range(1, 12):
                split(r, g, 0)
                split(r, g, 1)
                drain_ci(r, g - 1, (r["e0"] + g - 1) % 2)
                split(r, g, 2)
                split(r, g, 3)
            for c in range(4):
                act.wait_ge(s_lnr, c + 1)
                if c == 3:
                    act.wait_ge(s_lns, 2)
                nc.scalar.activation(conv_squares(c), yc_t[:, 1024 * c:1024 * c + 1024],
                                     ACT.Square).then_inc(s_lnq, 1)
                if c == 2:
                    drain_ci(r, 11, (r["e0"] + 11) % 2)
            presplit("co")
            act.wait_ge(s_lns, 5)
            nc.scalar.activation(sc[:, 0:T], bank[6][:, 0:T], ACT.Sqrt, bias=EPSB, scale=1.0 / D)\
                .then_inc(s_cvr, 1)
            for kt in range(KT):
                if kt % 4 == 0:
                    act.wait_ge(s_lny, kt // 4 + 1)
                nc.scalar.activation(yc[:, kt, :], yc[:, kt, :], ACT.Silu, bias=col("conv_ln_b_2", kt),
                                     scale=col("conv_ln_g_2", kt)).then_inc(s_lnz, 1)
            fill_u("yco", yc_t, "co", ready=lambda c: (s_yc, c + 1))
            run(RUN["co"], nothing, early="f3i")
            fourier("3", 2)
            norm("end")

        @block.vector
        def _(dve):
            v = nc.vector
            steps = [0]

            def link(ins):
                steps[0] += 1
                ins.then_inc(s_dv, 1)
                dve.wait_ge(s_dv, steps[0])

            def split(r, g, s):
                n = r["width"]
                dve.wait_ge(s_hi, g * SLABS + (SLABS * r["m0"] + s + 1))
                v.tensor_tensor(wlo[:, s, 0:n], raw[:, s, 0:n], whi[:, s % 2, 0:n].bitcast(F32),
                                ALU.subtract).then_inc(s_lo, 1)

            def presplit(name, g=0):
                split(RUN[name], g, 0)
                split(RUN[name], g, 1)

            def summed(r, g):
                dve.wait_ge(s_slab, (g + (r["m0"] + 1)) * SLABS)

            def ada_half(a, i, both):
                at = ada_at(a, both)
                first = isinstance(a, int) and a == 0
                dve.wait_ge(s_araw[i % 2], a * 64 + 16 * (i // 2 + 1))

                def step(n, out, kt, c, before):
                    if n == 0 and not both:
                        dve.wait_ge(s_acc, at)
                    elif not (first and n < 2):
                        dve.wait_ge(s_acc, at + (n - 1 if both else max(n - 1, 0)))
                    x = aslab[:, i % 2, kt % 2, :]
                    silu = sm[:, SM_SIL + 2 * kt + c:SM_SIL + 2 * kt + c + 1]
                    if before is None:
                        ins = v.tensor_scalar(out, x, silu, None, ALU.mult)
                    else:
                        ins = v.scalar_tensor_tensor(out=out, in0=x, scalar=silu, in1=before,
                                                     op0=ALU.mult, op1=ALU.add)
                    ins.then_inc(s_acc, 1)
                for kt in (2 * i, 2 * i + 1):
                    if both:
                        if kt == KT - 1 and not first:
                            dve.wait_ge(s_ada, a)
                        for c in range(2):
                            step(2 * kt + c, asum[:, c, :] if kt == KT - 1 else acc[:, c, :], kt, c,
                                 acc[:, c, :] if kt else None)
                    else:
                        step(kt, acc[:, kt % 2, :], kt, 0, acc[:, kt % 2, :] if kt >= 2 else None)
                if i == 7 and not both:
                    dve.wait_ge(s_acc, at + 16)
                    dve.wait_ge(s_ada, a)
                    v.tensor_tensor(asum[:, 0, :], acc[:, 0, :], acc[:, 1, :], ALU.add).then_inc(s_acc, 1)

            def run(r, drain, g0=0, n=None, then=None, early=None):
                n = r["n"] if n is None else n
                both = ada_both(r, g0)

                def ada_part(g, pair, odd, part, single=False):
                    if r["ada"] == 2:
                        ada_half(g + r["a0"], 2 * part, both)
                        ada_half(g + r["a0"], 2 * part + 1, both)
                    elif r["ada"] and not single:
                        ada_half(pair + r["a0"], 4 * odd + part, both)

                def group(g, pair, odd, before, single=False):
                    if before is not None:
                        split(r, g, 0)
                        ada_part(g, pair, odd, 0, single)
                        split(r, g, 1)
                        drain(r, *before)
                        ada_part(g, pair, odd, 1, single)
                        split(r, g, 2)
                        ada_part(g, pair, odd, 2, single)
                        split(r, g, 3)
                        ada_part(g, pair, odd, 3, single)
                    else:
                        split(r, g, 2)
                        ada_part(g, pair, odd, 0, single)
                        ada_part(g, pair, odd, 1, single)
                        split(r, g, 3)
                        ada_part(g, pair, odd, 2, single)
                        ada_part(g, pair, odd, 3, single)
                group(g0, g0 // 2, 0, None)
                pairs = (n - 1) // 2
                if pairs > 1:
                    with dve.Fori(0, pairs) as j:
                        for half in range(2):
                            group(j * 2 + (g0 + 1 + half), j + (g0 + 1 + half) // 2, 1 - half,
                                  (j * 2 + (g0 + half), (r["e0"] + g0 + half) % 2))
                else:
                    for g in range(g0 + 1, g0 + 1 + 2 * pairs):
                        group(g, g // 2, g % 2, (g - 1, (r["e0"] + g - 1) % 2), g - g0 >= n // 2 * 2)
                if (n - 1) % 2:
                    g = g0 + n - 1
                    group(g, g // 2, g % 2, (g - 1, (r["e0"] + g - 1) % 2))
                if then is not None:
                    presplit(*then)
                if early is not None:
                    split(RUN[early], 0, 0)
                drain(r, g0 + n - 1, (r["e0"] + g0 + n - 1) % 2)

            def nothing(r, g, par):
                pass

            def adder(dest_t, gate):
                def drain(r, g, par):
                    summed(r, g)
                    if gate is None:
                        for half in range(2):
                            at = 1024 * g + 512 * half
                            last = v.tensor_tensor(dest_t[:, at:at + 512], bank[2 * par + half][:, :],
                                                   dest_t[:, at:at + 512], ALU.add)
                    else:
                        for b in range(4):
                            at = 1024 * g + T * b
                            last = v.scalar_tensor_tensor(
                                out=dest_t[:, at:at + T],
                                in0=bank[2 * par + b // 2][:, T * (b % 2):T * (b % 2) + T],
                                scalar=gate(4 * g + b), in1=dest_t[:, at:at + T],
                                op0=ALU.mult, op1=ALU.add)
                    last.then_inc(s_drain, 2)
                return drain

            def norm(name):
                n = NORMS[name]
                src = NORM_ARGS[name][0]
                source_ready(dve, name)
                dve.wait_ge(s_rt, n + 1)
                rr = sc[:, 1024:1024 + T]
                link(v.reciprocal(rr, rr))
                if name in ("fin", "end"):
                    dest, signal = (hh, s_fin) if name == "fin" else (zf, s_yd)
                    for kt in range(KT):
                        last = v.scalar_tensor_tensor(out=dest[:, kt, :], in0=src[:, kt, :],
                                                      scalar=norm_scale(name, kt), in1=rr,
                                                      op0=ALU.mult, op1=ALU.mult)
                        if kt % 4 == 3:
                            last.then_inc(signal, 1)
                    return

                def lo(kt):
                    dve.wait_ge(s_nh, 16 * U_NORMS[name] + kt + 1)
                    sh = norm_shift(name, kt)
                    if sh is None:
                        last = v.tensor_tensor(ulo[:, kt, :], tt4[:, kt % 4, :],
                                               uhi[:, kt, :].bitcast(F32), ALU.subtract)
                    else:
                        last = v.scalar_tensor_tensor(out=ulo[:, kt, :], in0=tt4[:, kt % 4, :],
                                                      scalar=sh, in1=uhi[:, kt, :].bitcast(F32),
                                                      op0=ALU.add, op1=ALU.subtract)
                    last.then_inc(s_nl, 1)
                for kt in range(KT):
                    if kt >= 4:
                        dve.wait_ge(s_nl, 16 * U_NORMS[name] + kt - 3)
                    v.scalar_tensor_tensor(out=tt4[:, kt % 4, :], in0=src[:, kt, :],
                                           scalar=norm_scale(name, kt), in1=rr,
                                           op0=ALU.mult, op1=ALU.mult).then_inc(s_nt, 1)
                    if kt >= 2:
                        lo(kt - 2)
                    if kt == 5 and name != "nci":
                        split(RUN[AFTER_NORM[name]], 0, 1)
                lo(KT - 2)
                lo(KT - 1)

            def fill_u(name, src, chunks=4, width=1024, inc=1):
                for c in range(chunks):
                    dve.wait_ge(s_uh, 4 * SPLITS[name] + c + 1)
                    v.tensor_tensor(ulo_t[:, width * c:width * (c + 1)], src[:, width * c:width * (c + 1)],
                                    uhi_t[:, width * c:width * (c + 1)].bitcast(F32),
                                    ALU.subtract).then_inc(s_ul, inc)

            def ropes(jobs, base_job, table, first=0, between=()):
                def sums(i):
                    x, _, nb = jobs[i]
                    r = pt[:, 512 * (i % 2):512 * (i % 2) + T * nb]
                    dve.wait_ge(s_dv, need[i])
                    v.tensor_tensor(x, x, r, ALU.add).then_inc(s_ro, 1)
                need = {}
                for i in range(first, len(jobs)):
                    x, kind, nb = jobs[i]
                    cos, sin = table(kind, nb)
                    r = pt[:, 512 * (i % 2):512 * (i % 2) + T * nb]
                    dve.wait_ge(s_rm, base_job + i + 1)
                    if i >= 2:
                        dve.wait_ge(s_ro, base_job + i - 1)
                    as3 = lambda a, nb=nb: a.rearrange("p (k n) -> p k n", k=nb)
                    v.tensor_tensor(as3(r), as3(bank[5 + i % 3][:, 0:T * nb]), sin, ALU.mult)
                    v.tensor_tensor(as3(x), as3(x), cos, ALU.mult).then_inc(s_dv, 1)
                    steps[0] += 1
                    need[i] = steps[0]
                    if i > first:
                        sums(i - 1)
                    for job, slab in between:
                        if job == i:
                            slab()
                sums(len(jobs) - 1)

            def softmax_units(first, n, maxes, scales, outs):
                for t in range(n + 3):
                    units = []
                    if t < n:
                        units.append(maxes(t, first + t))
                    if 1 <= t <= n:
                        units.append(scales(t - 1, first + t - 1))
                    while units:
                        units = [u for u in units if next(u, None) is not None]
                    if t >= 3:
                        outs(t - 3, TN[first + t - 3])

            def score_slot(t, u):
                dve.wait_ge(s_s, u + 1)
                if t >= 3:
                    dve.wait_ge(s_t, TN[u - 3])
                    dve.wait_ge(s_pr, u - 1)

            def mark(ins):
                steps[0] += 1
                ins.then_inc(s_dv, 1)
                return steps[0]

            dve.wait_ge(s_in, 16 * INPUT_DMAS)
            lv = lamr[:, :].rearrange("p (l q n) -> p l q n", l=2, q=4)
            lp = sq[:, 0:256].rearrange("p (l q n) -> p l q n", l=2, q=2)
            for l in range(2):
                last = v.tensor_tensor(lp[:, l], lv[:, l, 0:4:2], lv[:, l, 1:4:2], ALU.mult)
            link(last)
            v.tensor_reduce(sm[:, SM_TMP:SM_TMP + 4], sq[:, 0:256].rearrange("p (a n) -> p a n", n=64),
                            AX.X, ALU.add).then_inc(s_lam, 1)
            link(v.tensor_copy(ang[:, 0:T], posi[:, :]))
            for k in (2, 1, 0):
                last = v.tensor_scalar(ang[:, T * k:T * (k + 1)], ang[:, 0:T],
                                       kk[:, K_INVF + k:K_INVF + k + 1], None, ALU.mult)
            link(last)
            TWO_PI = 2 * math.pi
            C1 = 6.28125
            C2 = float(np.float32(np.round((TWO_PI - C1) * 2 ** 20) / 2 ** 20))
            C3 = TWO_PI - C1 - C2
            ROUND = 12582912.0
            PI32 = 3.1415925
            for i, (turn, back) in enumerate(((0.25, math.pi / 2), (0.0, 0.0))):
                link(v.tensor_scalar(trn[:, :], ang[:, :], 1 / TWO_PI, turn, ALU.mult, ALU.add))
                link(v.tensor_scalar(trn[:, :], trn[:, :], ROUND, None, ALU.add))
                link(v.tensor_scalar(trn[:, :], trn[:, :], -ROUND, None, ALU.add))
                if i:
                    dve.wait_ge(s_tab, 1)
                link(v.scalar_tensor_tensor(out=red[:, :], in0=trn[:, :], scalar=-C1, in1=ang[:, :],
                                            op0=ALU.mult, op1=ALU.add))
                link(v.scalar_tensor_tensor(out=red[:, :], in0=trn[:, :], scalar=-C2, in1=red[:, :],
                                            op0=ALU.mult, op1=ALU.add))
                link(v.scalar_tensor_tensor(out=red[:, :], in0=trn[:, :], scalar=-C3, in1=red[:, :],
                                            op0=ALU.mult, op1=ALU.add))
                link(v.tensor_scalar(red[:, :], red[:, :], back, PI32, ALU.add, ALU.min))
                v.tensor_scalar(red[:, :], red[:, :], -PI32, None, ALU.max).then_inc(s_sin, 1)
            dve.wait_ge(s_lam, 2)
            for l in range(2):
                a = SM_TMP + 4 + 2 * l
                link(v.tensor_tensor(sm[:, SM_LAM + l:SM_LAM + l + 1], sm[:, a + 1:a + 2], sm[:, a:a + 1],
                                     ALU.subtract))
                v.tensor_scalar(sm[:, SM_LAM + l:SM_LAM + l + 1], sm[:, SM_LAM + l:SM_LAM + l + 1],
                                -LAM_INIT[l], None, ALU.add)
                link(v.tensor_scalar(sm[:, SM_SUBG + l:SM_SUBG + l + 1], col("subln_g", l),
                                     1.0 - LAM_INIT[l], None, ALU.mult))
            dve.wait_ge(s_tab, 2)

            def modulation(l):
                dve.wait_ge(s_ada, MOD_READS[l])
                conds = range(2 if l < 2 else 1)
                for c in conds:
                    at = 4 * ADA_GROUPS * c + 48 * l
                    last = v.tensor_tensor(mods[:, l, c, :], bank[4][:, at:at + 48],
                                           col("ada_b_2", 48 * l, 48), ALU.add)
                link(last)
                for c in conds:
                    last = v.scalar_tensor_tensor(out=gs[:, 32 * l + 16 * c:32 * l + 16 * c + 16],
                                                  in0=mods[:, l, c, 16:32], scalar=1.0,
                                                  in1=col("norm_g_2", 16 * l, 16),
                                                  op0=ALU.add, op1=ALU.mult)
                last.then_inc(s_mod, 1)
                dve.wait_ge(s_mod, l + 1)

            def first_block(l):
                if l == 0:
                    split(RUN["in0"], 0, 0)
                norm(f"n{l}")
                run(RUN[f"in{l}"], nothing, then=(f"v{l}",))
                run(RUN[f"v{l}"], nothing)
                dve.wait_ge(s_crt, l + 1)
                link(v.reciprocal(sc[:, 0:512], sc[:, 0:512]))
                for k in range(5):
                    g = col("q_norm_g", 3 * l + k) if k < 3 else col("kv_norm_g", 2 * l + k - 3)
                    last = v.scalar_tensor_tensor(out=sq[:, T * k:T * (k + 1)], in0=zz[:, Z_CQ + k, :],
                                                  scalar=g, in1=sc[:, T * (k > 2):T * (k > 2) + T],
                                                  op0=ALU.mult, op1=ALU.mult)
                last.then_inc(s_ct, 1)
                dve.wait_ge(s_ch, l + 1)
                v.tensor_tensor(cql[:, :, :], sq[:, 0:5 * T].rearrange("p (k n) -> p k n", n=T),
                                cqh[:, :, :].bitcast(F32), ALU.subtract).then_inc(s_cl, 1)

                def table(kind, nb):
                    return [tabs[:, 2 * kind + i:2 * kind + i + 1, :].broadcast_to([P, nb, T])
                            for i in range(2)]
                jobs = rope_jobs()
                r = RUN[f"up{l}"]
                split(r, 0, 0)
                split(r, 0, 1)
                ropes(jobs[:14], NJ * l, table, 0,
                      ((4, lambda: split(r, 0, 2)), (10, lambda: split(r, 0, 3))))
                dve.wait_ge(s_drain, 2 * (r["e0"] + 6))
                ropes(jobs, NJ * l, table, 14)
                acc = [sq[:, 1024 + T * t:1024 + T * (t + 1)] for t in range(2)]
                for h in range(8):
                    dve.wait_ge(s_ir, 8 * l + h + 1)
                    if h:
                        dve.wait_ge(s_ia, 16 * l + 2 * h)
                    for t in range(2):
                        x = pts[:, h % 2, T * t:T * (t + 1)]
                        wcol = vv[:, t, V_W + h:V_W + h + 1]
                        if h == 0:
                            ins = v.tensor_scalar(acc[t], x, wcol, None, ALU.mult)
                        else:
                            ins = v.scalar_tensor_tensor(out=acc[t], in0=x, scalar=wcol, in1=acc[t],
                                                         op0=ALU.mult, op1=ALU.add)
                        ins.then_inc(s_ia, 1)
                dve.wait_ge(s_ia, 16 * l + 16)
                work = sq[:, 512:1024]
                link(v.tensor_tensor(work, sq[:, 1024:1536], mask1, ALU.add))
                for i in range(TOPK // 8):
                    m8 = [sm[:, SM_M8 + 8 * t:SM_M8 + 8 * t + 8] for t in range(2)]
                    for t in range(2):
                        last = v.max(m8[t], work[:, T * t:T * (t + 1)])
                    link(last)
                    for t in range(2):
                        x = work[:, T * t:T * (t + 1)]
                        last = v.match_replace(x, m8[t], x, TAKEN)
                    link(last)
                bm = sq[:, 0:512]
                link(v.tensor_scalar(bm, work, TAKEN / 2, NEG, ALU.is_gt, ALU.mult))
                link(v.tensor_tensor(bm, bm, mask1, ALU.add))

                def maxes(i, u):
                    m = UNITS1[i][0]
                    x = scs[:, i % 3, :]
                    score_slot(i, u)
                    scale = {"a": 192 ** -0.5, "b": P ** -0.5, "c": 64 ** -0.5}[m]
                    v.scalar_tensor_tensor(out=x, in0=bank[i % 2][:, :], scalar=scale,
                                           in1=bm if m == "b" else mask1, op0=ALU.mult,
                                           op1=ALU.add).then_inc(s_sd, 1)
                    yield True
                    dve.wait_ge(s_sd, u + 1)
                    c = SM_NM + 2 * (i % 4)
                    v.tensor_reduce(sm[:, c:c + 2], x.rearrange("p (t n) -> p t n", t=2), AX.X, ALU.max,
                                    negate=True).then_inc(s_m, 1)

                def scales(i, u):
                    m, h, part = UNITS1[i]
                    c = 2 * (i % 4)
                    ri = sm[:, SM_RI + c:SM_RI + c + 2]
                    dve.wait_ge(s_e, u + 1)
                    done = mark(v.reciprocal(ri, sm[:, SM_SUM + c:SM_SUM + c + 2]))
                    yield True
                    x = scs[:, i % 3, :].rearrange("p (t n) -> p t n", t=2)
                    dve.wait_ge(s_dv, done)
                    if part == 0:
                        v.tensor_tensor(x, x, ri.unsqueeze(2).broadcast_to([P, 2, T]), ALU.mult)\
                            .then_inc(s_pr, 1)
                        return
                    rl = sm[:, SM_RL + c:SM_RL + c + 2]
                    link(v.tensor_scalar(rl, ri, sm[:, SM_LAM + l:SM_LAM + l + 1], None, ALU.mult))
                    for t in range(2):
                        last = v.scalar_tensor_tensor(out=x[:, t], in0=x[:, t], scalar=rl[:, t:t + 1],
                                                      in1=scs[:, (i - 1) % 3, T * t:T * (t + 1)],
                                                      op0=ALU.mult, op1=ALU.add)
                    last.then_inc(s_pr, 1)

                def outs(i, tn):
                    m, h, part = UNITS1[i]
                    if not HAS_T1[i]:
                        return
                    dve.wait_ge(s_o, tn)
                    o = bank[5 + (tn - 1) % 2][:, 0:T]
                    if m == "c":
                        v.tensor_copy(zz[:, Z_CQ + h, :], o).then_inc(s_of, 1)
                    else:
                        g = zz[:, h if m == "a" else 6 + h, :]
                        v.tensor_tensor(g, o, g, ALU.mult).then_inc(s_of, 1)
                dve.wait_ge(s_gate, l + 1)
                softmax_units(N1 * l, N1, maxes, scales, outs)
                presplit(f"ple{l}")
                fill_u(f"p{l}", praw[:, :, :].rearrange("p k n -> p (k n)"), 1, 512, 4)
                r = RUN[f"ple{l}"]
                dve.wait_ge(s_ort, l + 1)
                link(v.reciprocal(sc[:, 0:640], sc[:, 0:640]))
                split(r, 0, 2)
                link(v.reciprocal(sc[:, 640:1280], sc[:, 640:1280]))
                split(r, 0, 3)
                oc = zz_t[:, T * Z_CQ:T * (Z_CQ + 5)]
                link(v.scalar_tensor_tensor(out=oc, in0=oc, scalar=sm[:, SM_SUBG + l:SM_SUBG + l + 1],
                                            in1=sc[:, 0:5 * T], op0=ALU.mult, op1=ALU.mult))
                gc = zz_t[:, T * 11:T * 16]
                v.tensor_tensor(gc, gc, oc, ALU.mult).then_inc(s_mix, 1)
                presplit(f"o{l}")
                fill_u(f"m{l}", zz_t)
                run(RUN[f"o{l}"], adder(h_t, None), then=(f"pg{l}",))
                fill_u(f"g{l}", h_t)

                def drain_pg(r, g, par):
                    i = GATED[f"pg{l}"] + g
                    dve.wait_ge(s_drain, 2 * (r["e0"] + g + 1))
                    x = sq[:, 1024 * (i % 2):1024 * (i % 2) + 1024]
                    link(v.tensor_tensor(x, x, zz_t[:, T * 16 + 1024 * g:T * 16 + 1024 * g + 1024],
                                         ALU.mult))
                    y = h_t[:, 1024 * g:1024 * g + 1024]
                    v.tensor_tensor(y, y, x, ALU.add).then_inc(s_gu, 1)
                run(RUN[f"pg{l}"], drain_pg, early=("in1", "fci")[l])

            def fourier(tag, inv, dest_t, l, cond):
                r = RUN[f"f{tag}i"]
                norm("nf" + tag)
                run(r, nothing, 0, 4, then=(f"f{tag}i", 4))
                for g in range(8):
                    dve.wait_ge(s_f2, 8 * inv + g + 1)
                    v.tensor_copy(zf_t[:, 512 * g:512 * g + 512], bank[7][:, :]).then_inc(s_fb, 1)
                dve.wait_ge(s_fb, 8 * inv + 8)

                def drain_z(r, g, par):
                    i = GATED["f" + tag] + g - 4
                    dve.wait_ge(s_drain, 2 * (r["e0"] + g + 1))
                    y = zf_t[:, 1024 * (g - 4):1024 * (g - 4) + 1024]
                    v.tensor_tensor(y, y, sq[:, 1024 * (i % 2):1024 * (i % 2) + 1024], ALU.mult)\
                        .then_inc(s_gu, 1)
                run(r, drain_z, 4, 4, then=(f"f{tag}o",))
                fill_u("yf" + tag, zf_t)
                run(RUN[f"f{tag}o"], adder(dest_t, lambda b: mods[:, l, cond, 32 + b:33 + b]),
                    early={"c": "fxi", "x": "kc"}.get(tag))

            for l in range(2):
                first_block(l)
            modulation(0)
            norm("fin")
            fourier("c", 0, cc_t, 0, 1)
            fourier("x", 1, h_t, 0, 0)
            modulation(1)
            norm("nkc")
            run(RUN["kc"], nothing, then=("vc",))
            run(RUN["vc"], nothing, early="kx")
            norm("nx1")
            run(RUN["kx"], nothing, then=("vx",))
            run(RUN["vx"], nothing, then=("qz",))
            run(RUN["qz"], nothing)
            dve.wait_ge(s_drain, 2 * (RUN["qz"]["e0"] + 8))

            def table(kind, nb):
                return [k2[:, K2_AX + T * i:K2_AX + T * (i + 1)].unsqueeze(1).broadcast_to([P, nb, T])
                        for i in range(2)]
            ropes(rope_jobs_x(), 2 * NJ, table)
            nsink = lamr[:, 0:32]
            link(v.tensor_scalar(nsink, sinkr[:, :], -1.0, None, ALU.mult))

            def maxes(i, u):
                _, h, b = UNITS2[i]
                x = scs[:, i % 3, :]
                score_slot(i, u)
                v.scalar_tensor_tensor(out=x, in0=bank[i % 2][:, :], scalar=0.125, in1=mask2[:, b],
                                       op0=ALU.mult, op1=ALU.add).then_inc(s_sd, 1)
                yield True
                dve.wait_ge(s_sd, u + 1)
                c = SM_NM + 2 * (i % 4)
                done = mark(v.tensor_reduce(sm[:, c:c + 1], x, AX.X, ALU.max, negate=True))
                yield True
                dve.wait_ge(s_dv, done)
                v.tensor_tensor(sm[:, c:c + 1], sm[:, c:c + 1], nsink[:, h:h + 1], ALU.min)\
                    .then_inc(s_m, 1)

            def scales(i, u):
                c = 2 * (i % 4)
                ri = sm[:, SM_RI + c:SM_RI + c + 1]
                dve.wait_ge(s_e, u + 1)
                done = mark(v.tensor_tensor(ri, sm[:, SM_SUM + c:SM_SUM + c + 1],
                                            sm[:, SM_ES + i % 4:SM_ES + i % 4 + 1], ALU.add))
                yield True
                dve.wait_ge(s_dv, done)
                done = mark(v.reciprocal(ri, ri))
                yield True
                dve.wait_ge(s_dv, done)
                x = scs[:, i % 3, :]
                v.tensor_scalar(x, x, ri, None, ALU.mult).then_inc(s_pr, 1)

            def outs(i, tn):
                if i % 4 != 3:
                    return
                dve.wait_ge(s_o, tn)
                hp = i // 4
                g = zq[:, 16 + hp, :]
                v.tensor_tensor(g, bank[5 + hp % 2][:, 0:T], g, ALU.mult).then_inc(s_of, 1)
            dve.wait_ge(s_gate, 3)
            softmax_units(2 * N1, N2, maxes, scales, outs)
            modulation(2)
            presplit("ao")
            fill_u("ya", zq_t[:, 16 * T:32 * T])
            run(RUN["ao"], adder(h_t, lambda b: mods[:, 1, 0, 32 + b:33 + b]))
            v.memset(gp[:, :, 0:15], 0.0)
            link(v.memset(gp[:, :, 15 + T:PADT], 0.0))
            norm("nci")
            r = RUN["ci"]
            TAPS = 31

            def conv_steps():
                for k in range(0, KT, 2):
                    for t in range(TAPS):
                        for b in (k, k + 1):
                            x = gp[:, b, t:t + T]
                            wt = col("conv_dw_w_2", 16 * t + b)
                            yield b, t, x, wt
            conv = conv_steps()

            def conv_some(n):
                for _ in range(n):
                    s = next(conv, None)
                    if s is None:
                        return
                    b, t, x, wt = s
                    if t == 0:
                        if b % 2 == 0:
                            dve.wait_ge(s_drain, 2 * (r["e0"] + b // 2 + 1))
                        ins = v.tensor_scalar(yc[:, b, :], x, wt, col("conv_dw_b_2", b), ALU.mult, ALU.add)
                    else:
                        dve.wait_ge(s_dv, steps[0] - (0 if t == TAPS - 1 and b % 2 else 1))
                        ins = v.scalar_tensor_tensor(out=yc[:, b, :], in0=x, scalar=wt, in1=yc[:, b, :],
                                                     op0=ALU.mult, op1=ALU.add)
                    if (b, t) == (KT - 2, 0):
                        ins.then_inc(s_cb, 1)
                        dve.wait_ge(s_cb, 1)
                    elif t < TAPS - 1:
                        steps[0] += 1
                        ins.then_inc(s_dv, 1)
                    else:
                        ins.then_inc(s_conv, 1)

            def drain_ci(g):
                par = (r["e0"] + g) % 2
                dve.wait_ge(s_cg, g + 1)
                v.tensor_tensor(gp[:, 2 * g:2 * g + 2, 15:15 + T],
                                bank[2 * par][:, :].rearrange("p (k n) -> p k n", k=2),
                                sq[:, 1024 * (g % 2):1024 * (g % 2) + 512]
                                .rearrange("p (k n) -> p k n", k=2), ALU.mult).then_inc(s_drain, 2)
            for g in range(8):
                drain_ci(g)
                conv_some(2 * TAPS)
            dve.wait_ge(s_lns, 1)
            mu = sc[:, 512:768]
            link(v.tensor_scalar(mu, bank[5][:, 0:T], 1.0 / D, None, ALU.mult))
            mu4 = mu.unsqueeze(1).broadcast_to([P, 4, T])
            for c in range(4):
                y = yc[:, 4 * c:4 * c + 4, :]
                v.tensor_tensor(y, y, mu4, ALU.subtract).then_inc(s_lnr, 1)
            dve.wait_ge(s_lo, SLABS * (r["m0"] + 12))
            presplit("co")
            dve.wait_ge(s_cvr, 1)
            link(v.reciprocal(sc[:, 0:T], sc[:, 0:T]))
            r4 = sc[:, 0:T].unsqueeze(1).broadcast_to([P, 4, T])
            dve.wait_ge(s_lnr, 4)
            for c in range(4):
                y = yc[:, 4 * c:4 * c + 4, :]
                v.tensor_tensor(y, y, r4, ALU.mult).then_inc(s_lny, 1)
            for c in range(4):
                dve.wait_ge(s_lnz, 4 * c + 4)
                if c == 0:
                    dve.wait_ge(s_drain, 2 * (r["e0"] + 12))
                y = yc_t[:, 1024 * c:1024 * c + 1024]
                v.tensor_tensor(y, y, zs_t[:, 1024 * c:1024 * c + 1024], ALU.mult).then_inc(s_yc, 1)

            fill_u("yco", yc_t)
            run(RUN["co"], adder(h_t, lambda b: mods[:, 2, 0, 32 + b:33 + b]), early="f3i")
            modulation(3)
            fourier("3", 2, h_t, 3, 0)
            norm("end")


def slabs_of(w, col_blocks):
    w = np.asarray(w)
    n = len(col_blocks)
    assert n % 4 == 0
    out = np.zeros((n // 4, SLABS, P, 4, 4, P), w.dtype)
    v = w.reshape(SLABS, 4, P, w.shape[1])
    for b, c in enumerate(col_blocks):
        if c is None:
            continue
        pieces = c if isinstance(c, list) else [(c, P)]
        at = 0
        for c0, m in pieces:
            out[b // 4, :, :, :, b % 4, at:at + m] = v[:, :, :, c0:c0 + m].transpose(0, 2, 1, 3)
            at += m
    return out.reshape(n // 4, SLABS, P, 2048)


def tiles_of(tiles, dtype):
    out = np.zeros((SLABS, P, 16, P), dtype)
    for i, t in enumerate(tiles):
        if t is not None:
            out[i // 16, :, i % 16, :] = t
    return out.reshape(SLABS, P, 2048)


def run_of(c0, n):
    return [c0 + P * i for i in range(n)]


def host_weights(a):
    out = {}
    win, wv, wup, wple = [], [], [], []
    for l in range(2):
        w = a["w_in"][l]
        blocks = (run_of(704, 6) + run_of(3976, 5) + run_of(6536, 5)
                  + run_of(1472, 5) + run_of(2112, 5) + run_of(3392, 4) + [[(3904, 64), (3904, 64)]]
                  + run_of(4616, 5) + run_of(5256, 5) + run_of(0, 5) + [[(640, 64), (640, 64)]] + [None])
        win.append(slabs_of(w, blocks))
        vb = run_of(2752, 5) + [[(3968, 8), (5896, 120)]] + run_of(5896 + 120, 4) + [[(6528, 8)]] + [None]
        wv.append(slabs_of(w, vb))
        q = a["w_uq"][l].reshape(3, P, 1152)
        kv = a["w_ukv"][l].reshape(2, P, 1536)
        t = []
        qcols = [[(192 * h, P)] for h in range(6)]
        qcols += [[(192 * h + P, 64), (192 * (h + 1) + P, 64)] for h in (0, 2, 4)]
        for b in range(9):
            for k in range(3):
                t.append(np.concatenate([q[k][:, c:c + n] for c, n in qcols[b]], axis=1))
            if b == 4:
                t.append(None)
        for h in range(6):
            for k in range(2):
                t.append(kv[k][:, T * h:T * h + P])
        for h0, h1 in ((0, 4), (4, 6)):
            for k in range(2):
                for h in range(h0, h1):
                    t.append(kv[k][:, T * h + P:T * h + 2 * P])
        wup.append(tiles_of(t, q.dtype)[None])
        e = a["w_ple"][l].reshape(2, P, 4, 4, P)
        ple = np.zeros((SLABS, P, 16, P), e.dtype)
        ple[:, :, 0:8, :] = e.transpose(2, 1, 0, 3, 4).reshape(SLABS, P, 8, P)
        wple.append(ple.reshape(1, SLABS, P, 2048))
    out["win"], out["wv"] = np.concatenate(win), np.concatenate(wv)
    out["wup"], out["wple"] = np.concatenate(wup), np.concatenate(wple)
    full = run_of(0, 16)
    out["wo"] = np.concatenate([slabs_of(a["w_o"][l], full) for l in range(2)])
    out["wpg"] = np.concatenate([slabs_of(a["w_pg"][l], full) for l in range(2)])
    out["ada"] = np.concatenate([slabs_of(a["ada_w_2"][l], run_of(0, 48)) for l in range(4)])
    out["wfi"] = np.concatenate([slabs_of(a["four_w_in_2"][l], run_of(0, 32)) for l in range(2)])
    out["wfo"] = np.concatenate([slabs_of(a["four_w_out_2"][l], full) for l in range(2)])
    w = a["attn_w_in_2"][0]
    out["wk"] = slabs_of(w, [[(2048 + 64 * j, 64), (2048 + 64 * j, 64)] for j in range(4)])
    out["wvx"] = slabs_of(w, run_of(2304, 2) + [None, None])
    out["wqz"] = slabs_of(w, run_of(0, 16) + run_of(2560, 16))
    out["wao"] = slabs_of(a["attn_w_out_2"][0], full)
    ci = [c for g in range(8) for c in (256 * g, 256 * g + P, D + 256 * g, D + 256 * g + P)]
    out["wci"] = slabs_of(a["conv_w_in_2"][0], ci + run_of(2 * D, 16))
    out["wco"] = slabs_of(a["conv_w_out_2"][0], full)
    return out


def rotation(half, period):
    m = np.zeros((P, P), np.float32)
    for o in range(0, P, period):
        for i in range(half):
            m[o + i + half, o + i] = -1.0
            m[o + i, o + i + half] = 1.0
    return m


def host_constants():
    kk = np.zeros((P, K_N), np.float32)
    kk[:, K_ID:K_ID + P] = np.eye(P)
    for i, (half, period) in enumerate(((32, 64), (16, P), (8, 64), (16, 32))):
        kk[:, K_ROT + P * i:K_ROT + P * (i + 1)] = rotation(half, period)
    q, key = np.arange(P)[:, None], np.arange(T)[None, :]
    for t in range(2):
        seen = key // 64 <= (q + P * t) // 64
        kk[:, K_MASK + T * t:K_MASK + T * (t + 1)] = np.where(seen, 0.0, NEG)
    for i, (half, period) in enumerate(((32, 64), (16, P), (8, 64))):
        f = np.float32(1.0) / np.float32(500000.0) ** (np.arange(half, dtype=np.float32)
                                                      * np.float32(2.0 / (2 * half)))
        for o in range(0, P, period):
            kk[o:o + half, K_INVF + i] = f
            kk[o + half:o + 2 * half, K_INVF + i] = f
    k2 = np.zeros((P, K2_N), np.float32)
    n = np.arange(T)
    angle = 2 * np.pi * (n[:, None] * n[None, :] % T) / T
    for k in range(2):
        rows = slice(P * k, P * (k + 1))
        k2[:, 512 * k:512 * k + T] = np.cos(angle[rows]) / 16
        k2[:, 512 * k + T:512 * k + 512] = np.sin(angle[rows]) / 16
    inv = np.float32(10000.0) ** (-np.arange(16, dtype=np.float32) / np.float32(16))
    row, column = (n // 64).astype(np.float32), (n % 64).astype(np.float32)
    ar, ac = row[:, None] * inv[None, :], column[:, None] * inv[None, :]
    full = np.concatenate([ar, ar, ac, ac], axis=1)
    full = np.concatenate([full, full], axis=1).T
    k2[:, K2_AX:K2_AX + T] = np.cos(full.astype(np.float64))
    k2[:, K2_AX + T:K2_AX + 2 * T] = np.sin(full.astype(np.float64))
    for b in range(2):
        near = np.abs(q + P * b - key) <= 128
        k2[:, K2_MASK + 512 * b:K2_MASK + 512 * b + T] = np.where(near, 0.0, NEG)
    return kk, k2


def transposed(x):
    x = np.asarray(x)
    return np.ascontiguousarray(x.reshape(T, -1, P).transpose(2, 1, 0))


def kernel(**inputs):
    import concourse.bacc as bacc
    from concourse.bass_utils import run_bass_kernel_spmd

    a = {k: np.asarray(v) for k, v in inputs.items()}
    arrays = {"w_" + k: v for k, v in host_weights(a).items()}
    cols = np.concatenate([np.asarray(a[name]).reshape(-1, P) for name in COL], axis=0)
    assert cols.shape[0] == NCOL
    arrays["cols"] = np.ascontiguousarray(cols.T)
    arrays["x"] = transposed(a["x"][0])
    arrays["ctx"] = transposed(a["ctx_2"][0])
    arrays["p"] = np.stack([transposed(a["p"][l, 0]) for l in range(2)])
    lam = np.stack([np.stack([a[n][l] for n in ("lam_q1", "lam_k1", "lam_q2", "lam_k2")])
                    for l in range(2)])
    arrays["lam"] = np.ascontiguousarray(np.broadcast_to(lam.reshape(1, -1), (P, 512)))
    arrays["sink"] = np.ascontiguousarray(np.broadcast_to(a["attn_sink_2"].reshape(1, 32), (P, 32)))
    arrays["pos"] = np.ascontiguousarray(np.broadcast_to(a["positions"].reshape(1, T), (P, T)))
    arrays["eps"] = np.full((P, 1), EPS, np.float32)
    arrays["consts"], arrays["consts2"] = host_constants()

    nc = bacc.Bacc("TRN2", target_bir_lowering=False, num_devices=1)
    aps = {n: nc.dram_tensor(n + "_dram", v.shape, mybir.dt.from_np(v.dtype), kind="ExternalInput").ap()
           for n, v in arrays.items()}
    out = nc.dram_tensor("out_dram", (P, KT, T), F32, kind="ExternalOutput").ap()
    build(nc, {n[2:]: ap for n, ap in aps.items() if n.startswith("w_")}, aps, out)
    r = run_bass_kernel_spmd(nc, [{n + "_dram": v for n, v in arrays.items()}], core_ids=[0])
    got = r.results[0]["out_dram"]
    return np.ascontiguousarray(np.asarray(got).transpose(2, 1, 0)).reshape(1, T, D)
```
